# Optimizing a Trainium2 kernel written in Bass

```python
import math
import jax
import jax.numpy as jnp
from jax import lax
import numpy as np

D_MODEL = 1024
BATCH = 1
SEQ = 256
DEPTH = 1

D_MIX = 2 * D_MODEL
ML_HEADS = 4
ML_DV = D_MODEL // ML_HEADS
ML_DQK = ML_DV // 2
ML_QK = ML_HEADS * ML_DQK
ML_WIDTH = ML_HEADS * ML_DV
SSM_WIDTH = D_MIX - ML_WIDTH
SSM_HEADDIM = 64
SSM_HEADS = SSM_WIDTH // SSM_HEADDIM
SSM_GROUPS = 4
SSM_STATE = 128
SSM_CONV_DIM = SSM_WIDTH + 2 * SSM_GROUPS * SSM_STATE
CONV_K = 5
CHUNK = 128
N_EXPERTS = 64
TOP_K = 8
N_EXPERT_GROUPS = 8
TOPK_GROUPS = 4
D_EXPERT = D_MODEL // 4
ROUTED_SCALE = 2.5
MOE_BLOCK = 512
LN_EPS = 1e-5
RMS_EPS = 1e-5
ALPHA = (2 * DEPTH) ** 0.25
BETA = (8 * DEPTH) ** -0.25
IN_SIZES = (ML_QK, ML_QK, ML_WIDTH, ML_WIDTH, 2 * ML_HEADS, 2 * ML_HEADS, SSM_WIDTH, SSM_CONV_DIM, 2 * SSM_HEADS)
IN_SCALES = (D_MODEL ** -0.5,) * 8 + (0.1 * D_MODEL ** -0.5,)
IN_SPLITS = tuple(int(s) for s in np.cumsum(IN_SIZES)[:-1])
D_IN_PROJ = sum(IN_SIZES)

kernel_name = 'hymba_mlstm_mamba2_moe_encoder_block'

def _layer_norm(x, g, b):
    xf = x.astype(jnp.float32)
    mu = xf.mean(-1, keepdims=True)
    var = jnp.square(xf - mu).mean(-1, keepdims=True)
    return ((xf - mu) * lax.rsqrt(var + LN_EPS) * g + b).astype(x.dtype)

def _mlstm_chunkwise(q, k, v, i_pre, f_pre):
    Bb, H, S, Dk = q.shape
    Dv = v.shape[-1]
    nc = S // CHUNK
    q = q.reshape(Bb, H, nc, CHUNK, Dk)
    k = k.reshape(Bb, H, nc, CHUNK, Dk)
    v = v.reshape(Bb, H, nc, CHUNK, Dv)
    ig = i_pre.reshape(Bb, H, nc, CHUNK)
    b = jnp.cumsum(jax.nn.log_sigmoid(f_pre).reshape(Bb, H, nc, CHUNK), axis=-1)
    g = b[..., -1]
    a = g[..., None] - b + ig
    m_loc = a.max(-1)
    kw = k * jnp.exp(a - m_loc[..., None])[..., None]
    U = jnp.einsum('bhcsk,bhcsv->bhckv', kw, v)
    u = kw.sum(3)

    def step(carry, inp):
        C, n, m = carry
        U_c, u_c, g_c, ml_c = inp
        m_new = jnp.maximum(g_c + m, ml_c)
        decay = jnp.exp(g_c + m - m_new)
        scale = jnp.exp(ml_c - m_new)
        C_new = decay[..., None, None] * C + scale[..., None, None] * U_c
        n_new = decay[..., None] * n + scale[..., None] * u_c
        return (C_new, n_new, m_new), (C, n, m)

    init = (jnp.zeros((Bb, H, Dk, Dv), jnp.float32), jnp.zeros((Bb, H, Dk), jnp.float32),
            jnp.full((Bb, H), -jnp.inf, jnp.float32))
    mv = lambda t: jnp.moveaxis(t, 2, 0)
    _, (Cp, n_p, m_p) = lax.scan(step, init, (mv(U), mv(u), mv(g), mv(m_loc)))
    Cp = jnp.moveaxis(Cp, 0, 2)
    n_p = jnp.moveaxis(n_p, 0, 2)
    m_p = jnp.moveaxis(m_p, 0, 2)

    tril = jnp.tril(jnp.ones((CHUNK, CHUNK), bool))
    dmat = jnp.where(tril, b[..., :, None] - b[..., None, :] + ig[..., None, :], -jnp.inf)
    m_inter = b + m_p[..., None]
    m_t = jnp.maximum(m_inter, dmat.max(-1))
    s_mat = jnp.einsum('bhctk,bhcsk->bhcts', q, k) * jnp.exp(dmat - m_t[..., None])
    inter_w = jnp.exp(m_inter - m_t)
    num = jnp.einsum('bhcts,bhcsv->bhctv', s_mat, v) + inter_w[..., None] * jnp.einsum('bhctk,bhckv->bhctv', q, Cp)
    den = s_mat.sum(-1) + inter_w * jnp.einsum('bhctk,bhck->bhct', q, n_p)
    h = num / jnp.maximum(jnp.abs(den), jnp.exp(-m_t))[..., None]
    return h.reshape(Bb, H, S, Dv)

def _mlstm_group(q, k, v, o, i_pre, f_pre, i_bias, f_bias, norm_w):
    Bb, S, _ = q.shape
    H = ML_HEADS
    heads = lambda t, d: t.reshape(Bb, S, H, d).transpose(0, 2, 1, 3).astype(jnp.float32)
    qh = heads(q, ML_DQK)
    kh = heads(k, ML_DQK) * (ML_DQK ** -0.5)
    vh = heads(v, ML_DV)
    ig = (i_pre.astype(jnp.float32) + i_bias.astype(jnp.float32)).transpose(0, 2, 1)
    fg = (f_pre.astype(jnp.float32) + f_bias.astype(jnp.float32)).transpose(0, 2, 1)
    flip = lambda t: jnp.flip(t, axis=2)
    h_fwd = _mlstm_chunkwise(qh, kh, vh, ig[:, :H], fg[:, :H])
    h_bwd = flip(_mlstm_chunkwise(flip(qh), flip(kh), flip(vh), flip(ig[:, H:]), flip(fg[:, H:])))
    h = h_fwd + h_bwd
    mu = h.mean(-1, keepdims=True)
    var = jnp.square(h - mu).mean(-1, keepdims=True)
    h = (h - mu) * lax.rsqrt(var + LN_EPS) * norm_w.astype(jnp.float32).reshape(H, 1, ML_DV)
    h = h.transpose(0, 2, 1, 3).reshape(Bb, S, ML_WIDTH)
    return (jax.nn.sigmoid(o.astype(jnp.float32)) * h).astype(q.dtype)

def _ssd_chunked(x, dt, A, Bm, Cm):
    Bb, S, H, P = x.shape
    G, N = Bm.shape[2], Bm.shape[3]
    hg = H // G
    nc = S // CHUNK
    x = x.reshape(Bb, nc, CHUNK, G, hg, P)
    dt = dt.reshape(Bb, nc, CHUNK, G, hg)
    Bm = Bm.reshape(Bb, nc, CHUNK, G, N)
    Cm = Cm.reshape(Bb, nc, CHUNK, G, N)
    acum = jnp.cumsum(dt * A.reshape(G, hg), axis=2)
    xdt = x * dt[..., None]
    tril = jnp.tril(jnp.ones((CHUNK, CHUNK), bool))
    seg = acum[:, :, :, None] - acum[:, :, None, :]
    decay_ts = jnp.exp(jnp.where(tril[:, :, None, None], seg, -jnp.inf))
    cb = jnp.einsum('bctgn,bcsgn->bctsg', Cm, Bm)
    y_diag = jnp.einsum('bctsgh,bcsghp->bctghp', cb[..., None] * decay_ts, xdt)
    decay_s = jnp.exp(acum[:, :, -1:] - acum)
    states = jnp.einsum('bcsgn,bcsghp->bcghpn', Bm, xdt * decay_s[..., None])
    chunk_decay = jnp.exp(acum[:, :, -1])

    def step(h, inp):
        st, dc = inp
        return dc[..., None, None] * h + st, h

    _, h_prev = lax.scan(step, jnp.zeros((Bb, G, hg, P, N), jnp.float32),
                         (jnp.moveaxis(states, 1, 0), jnp.moveaxis(chunk_decay, 1, 0)))
    h_prev = jnp.moveaxis(h_prev, 0, 1)
    y_off = jnp.einsum('bctgn,bcghpn->bctghp', Cm, h_prev) * jnp.exp(acum)[..., None]
    return (y_diag + y_off).reshape(Bb, S, H, P)

def _mamba2_group(z, xbc, dt_pre, conv_w, conv_b, dt_bias, a_log, d_skip, norm_w):
    Bb, S, _ = z.shape
    H = SSM_HEADS
    xbc = lax.conv_general_dilated(xbc, conv_w[:, None, :], window_strides=(1,),
                                   padding=[(CONV_K // 2, CONV_K // 2)],
                                   dimension_numbers=('NWC', 'WIO', 'NWC'),
                                   feature_group_count=SSM_CONV_DIM) + conv_b
    xbc = jax.nn.silu(xbc)
    xs, Bm, Cm = jnp.split(xbc, [SSM_WIDTH, SSM_WIDTH + SSM_GROUPS * SSM_STATE], axis=-1)
    xs = xs.reshape(Bb, S, H, SSM_HEADDIM).astype(jnp.float32)
    Bm = Bm.reshape(Bb, S, SSM_GROUPS, SSM_STATE).astype(jnp.float32)
    Cm = Cm.reshape(Bb, S, SSM_GROUPS, SSM_STATE).astype(jnp.float32)
    dt = jax.nn.softplus(dt_pre.astype(jnp.float32) + dt_bias.astype(jnp.float32))
    A = -jnp.exp(a_log.astype(jnp.float32))
    fl = lambda t: jnp.flip(t, axis=1)
    y_f = _ssd_chunked(xs, dt[..., :H], A[:H], Bm, Cm)
    y_b = fl(_ssd_chunked(fl(xs), fl(dt[..., H:]), A[H:], fl(Bm), fl(Cm)))
    y = y_f + y_b + d_skip.astype(jnp.float32)[:, None] * xs
    y = y.reshape(Bb, S, SSM_WIDTH) * jax.nn.silu(z.astype(jnp.float32))
    yg = y.reshape(Bb, S, SSM_GROUPS, SSM_WIDTH // SSM_GROUPS)
    yg = yg * lax.rsqrt(jnp.mean(yg * yg, -1, keepdims=True) + RMS_EPS)
    return (yg.reshape(Bb, S, SSM_WIDTH) * norm_w.astype(jnp.float32)).astype(z.dtype)

def _moe(x2d, w_router, router_bias, w_gate, w_up, w_down, ws_gate, ws_up, ws_down):
    T, D = x2d.shape
    E = N_EXPERTS
    scores = jax.nn.sigmoid((x2d @ w_router).astype(jnp.float32))
    choice = scores + router_bias.astype(jnp.float32)
    grp_score = lax.top_k(choice.reshape(T, N_EXPERT_GROUPS, E // N_EXPERT_GROUPS), 2)[0].sum(-1)
    _, top_groups = lax.top_k(grp_score, TOPK_GROUPS)
    gmask = jnp.any(top_groups[..., None] == jnp.arange(N_EXPERT_GROUPS), axis=1)
    emask = jnp.repeat(gmask, E // N_EXPERT_GROUPS, axis=1)
    _, idx = lax.top_k(jnp.where(emask, choice, -jnp.inf), TOP_K)
    wsel = jnp.take_along_axis(scores, idx, axis=1)
    wsel = wsel / wsel.sum(-1, keepdims=True) * ROUTED_SCALE

    M = T * TOP_K
    e_flat = idx.reshape(M)
    tok_flat = jnp.arange(M, dtype=jnp.int32) // TOP_K
    g_flat = wsel.reshape(M)
    order = jnp.argsort(e_flat)
    e_sorted = e_flat[order]
    counts = jnp.bincount(e_flat, length=E)
    starts = jnp.cumsum(counts) - counts
    pcounts = (counts + MOE_BLOCK - 1) // MOE_BLOCK * MOE_BLOCK
    pends = jnp.cumsum(pcounts)
    pstarts = pends - pcounts
    dest = pstarts[e_sorted] + (jnp.arange(M, dtype=jnp.int32) - starts[e_sorted])
    nb = (M + E * (MOE_BLOCK - 1)) // MOE_BLOCK
    slot_tok = jnp.zeros((nb * MOE_BLOCK,), jnp.int32).at[dest].set(tok_flat[order])
    slot_gate = jnp.zeros((nb * MOE_BLOCK,), jnp.float32).at[dest].set(g_flat[order])
    block_expert = jnp.minimum(jnp.searchsorted(pends, jnp.arange(nb) * MOE_BLOCK, side='right'), E - 1)

    def body(y, blk):
        tok, gate, e = blk
        xb = x2d[tok]
        h = jax.nn.silu(xb @ w_gate[e]) * (xb @ w_up[e])
        out = (h @ w_down[e]) * gate[:, None].astype(x2d.dtype)
        return y.at[tok].add(out), None

    routed, _ = lax.scan(body, jnp.zeros_like(x2d),
                         (slot_tok.reshape(nb, MOE_BLOCK), slot_gate.reshape(nb, MOE_BLOCK), block_expert))
    shared = (jax.nn.silu(x2d @ ws_gate) * (x2d @ ws_up)) @ ws_down
    return routed + shared

def _layer(x, w_in, ml_i_bias, ml_f_bias, ml_norm_w, conv_w, conv_b, dt_bias, a_log, d_skip, ssm_norm_w,
           w_out, ln1_g, ln1_b, w_router, router_bias, w_exp_gate, w_exp_up, w_exp_down,
           w_sh_gate, w_sh_up, w_sh_down, ln2_g, ln2_b):
    Bb, S, D = x.shape
    proj = jnp.einsum('bsd,de->bse', x, w_in)
    q, k, v, o, ig, fg, z, xbc, dt = jnp.split(proj, IN_SPLITS, axis=-1)
    y_ml = _mlstm_group(q, k, v, o, ig, fg, ml_i_bias, ml_f_bias, ml_norm_w)
    y_ssm = _mamba2_group(z, xbc, dt, conv_w, conv_b, dt_bias, a_log, d_skip, ssm_norm_w)
    mix = jnp.einsum('bse,ed->bsd', jnp.concatenate([y_ml, y_ssm], axis=-1), w_out)
    h = _layer_norm(ALPHA * x + mix, ln1_g, ln1_b)
    ffn = _moe(h.reshape(Bb * S, D), w_router, router_bias, w_exp_gate, w_exp_up, w_exp_down,
               w_sh_gate, w_sh_up, w_sh_down).reshape(Bb, S, D)
    return _layer_norm(ALPHA * h + ffn, ln2_g, ln2_b)

def setup_inputs(seed: int = 0) -> dict:
    key = jax.random.key(seed)
    ks = jax.random.split(key, 32)
    f32 = jnp.float32
    L = DEPTH
    nrm = lambda kk, shape, scale: jax.random.normal(kk, shape, f32) * scale
    x = nrm(ks[0], (BATCH, SEQ, D_MODEL), 1.0)
    wk = jax.random.split(ks[1], len(IN_SIZES))
    w_in = jnp.concatenate([nrm(wk[j], (L, D_MODEL, IN_SIZES[j]), IN_SCALES[j]) for j in range(len(IN_SIZES))], axis=-1)
    ml_i_bias = nrm(ks[2], (L, 2 * ML_HEADS), 0.1)
    ml_f_bias = 3.0 + 3.0 * jax.random.uniform(ks[3], (L, 2 * ML_HEADS), f32)
    ml_norm_w = 1.0 + nrm(ks[4], (L, ML_WIDTH), 0.02)
    conv_w = nrm(ks[5], (L, CONV_K, SSM_CONV_DIM), CONV_K ** -0.5)
    conv_b = nrm(ks[6], (L, SSM_CONV_DIM), 0.02)
    dt0 = jnp.exp(jax.random.uniform(ks[7], (L, 2 * SSM_HEADS), f32, math.log(1e-3), math.log(1e-1)))
    dt_bias = dt0 + jnp.log(-jnp.expm1(-dt0))
    a_log = jnp.log(jax.random.uniform(ks[8], (L, 2 * SSM_HEADS), f32, 1.0, 16.0))
    d_skip = 1.0 + nrm(ks[9], (L, SSM_HEADS), 0.02)
    ssm_norm_w = 1.0 + nrm(ks[10], (L, SSM_WIDTH), 0.02)
    w_out = nrm(ks[11], (L, D_MIX, D_MODEL), D_MIX ** -0.5 * BETA)
    ln1_g = 1.0 + nrm(ks[12], (L, D_MODEL), 0.02)
    ln1_b = nrm(ks[13], (L, D_MODEL), 0.02)
    w_router = nrm(ks[14], (L, D_MODEL, N_EXPERTS), D_MODEL ** -0.5)
    router_bias = nrm(ks[15], (L, N_EXPERTS), 0.01)
    w_exp_gate = nrm(ks[16], (L, N_EXPERTS, D_MODEL, D_EXPERT), D_MODEL ** -0.5)
    w_exp_up = nrm(ks[17], (L, N_EXPERTS, D_MODEL, D_EXPERT), D_MODEL ** -0.5)
    w_exp_down = nrm(ks[18], (L, N_EXPERTS, D_EXPERT, D_MODEL), D_EXPERT ** -0.5 * BETA)
    w_sh_gate = nrm(ks[19], (L, D_MODEL, D_EXPERT), D_MODEL ** -0.5)
    w_sh_up = nrm(ks[20], (L, D_MODEL, D_EXPERT), D_MODEL ** -0.5)
    w_sh_down = nrm(ks[21], (L, D_EXPERT, D_MODEL), D_EXPERT ** -0.5 * BETA)
    ln2_g = 1.0 + nrm(ks[22], (L, D_MODEL), 0.02)
    ln2_b = nrm(ks[23], (L, D_MODEL), 0.02)
    return {'x': x, 'w_in': w_in, 'ml_i_bias': ml_i_bias, 'ml_f_bias': ml_f_bias, 'ml_norm_w': ml_norm_w,
            'conv_w': conv_w, 'conv_b': conv_b, 'dt_bias': dt_bias, 'a_log': a_log, 'd_skip': d_skip,
            'ssm_norm_w': ssm_norm_w, 'w_out': w_out, 'ln1_g': ln1_g, 'ln1_b': ln1_b,
            'w_router': w_router, 'router_bias': router_bias, 'w_exp_gate': w_exp_gate,
            'w_exp_up': w_exp_up, 'w_exp_down': w_exp_down, 'w_sh_gate': w_sh_gate,
            'w_sh_up': w_sh_up, 'w_sh_down': w_sh_down, 'ln2_g': ln2_g, 'ln2_b': ln2_b}

def reference(x, w_in, ml_i_bias, ml_f_bias, ml_norm_w, conv_w, conv_b, dt_bias, a_log, d_skip,
              ssm_norm_w, w_out, ln1_g, ln1_b, w_router, router_bias, w_exp_gate, w_exp_up, w_exp_down,
              w_sh_gate, w_sh_up, w_sh_down, ln2_g, ln2_b):
    for l in range(DEPTH):
        x = _layer(x, w_in[l], ml_i_bias[l], ml_f_bias[l], ml_norm_w[l], conv_w[l], conv_b[l], dt_bias[l],
                   a_log[l], d_skip[l], ssm_norm_w[l], w_out[l], ln1_g[l], ln1_b[l], w_router[l],
                   router_bias[l], w_exp_gate[l], w_exp_up[l], w_exp_down[l], w_sh_gate[l], w_sh_up[l],
                   w_sh_down[l], ln2_g[l], ln2_b[l])
    return x


_drawn_inputs = setup_inputs


def setup_inputs(seed=0):
    import zlib

    import numpy as np

    out = dict(_drawn_inputs(seed))
    spreads = {}
    factors = {'ml_i_bias': 7.338,
     'ml_norm_w': 3.116,
     'd_skip': 7.251,
     'ln2_g': 22.5,
     'ln2_b': 23.189,
     'ssm_norm_w': 2.747}
    for name, (base, spread) in spreads.items():
        noise = np.random.default_rng([zlib.crc32(name.encode()), seed]).standard_normal(out[name].shape)
        drawn = base * np.exp(spread * noise) if base else spread * noise
        out[name] = jnp.asarray(drawn.astype(out[name].dtype))
    for name, factor in factors.items():
        out[name] = (out[name] * factor).astype(out[name].dtype)
    return out
```

```python
from contextlib import ExitStack

import concourse.bass as bass
from concourse import mybir

F32 = mybir.dt.float32
BF16 = mybir.dt.bfloat16
ALU = mybir.AluOpType
ACT = mybir.ActivationFunctionType
AX_X = mybir.AxisListType.X

P = 128
D = 1024
S = 256
T = S // P
KD = D // P
H = 4
DV = D // H
DQK = DV // 2
SH = 16
G = 4
HP = 64
NST = 128
CH = D + 2 * G * NST
CT = CH // P
TAPS = 5
E = 64
EG = 8
TOPG = 4
TOPK = 8
FE = D // 4
ROUTED_SCALE = 2.5
EPS = 1e-5
ALPHA = 2 ** 0.25
R = 112
ROW0 = (0, 32, 64, 96)
NEG = -1.0e30
BIG = 1.0e30

KIB = 256
SLOT = 24 * KIB
O_RING = 0
O_XT = 72 * KIB
O_XPAD = 80 * KIB
O_XBC = O_XPAD + CT * (S + 4)
O_V = O_XBC + CT * S
O_QK = O_V + T * H * (DV + 1)
O_ST = O_QK + 8 * KIB
O_W = O_ST + 8 * KIB
O_OH = O_W + 24 * KIB
O_Z = O_OH + 8 * KIB
O_XS = O_Z + 8 * KIB
O_HML = O_XS + 8 * KIB
O_NRM = O_HML + 8 * KIB
O_ROWS = O_NRM + 8 * KIB
O_END = O_ROWS + 3 * KIB

BLOCKS = [(0, 0, 0, True), (0, 0, 1, False), (0, 1, 1, True),
          (1, 0, 0, True), (1, 1, 0, False), (1, 1, 1, True)]
NB = len(BLOCKS)
LOADS = 13
RING1 = 3
RING2 = 4
UNROLL = RING2
ITEMS = E + 1


def build(nc, a, out):
    ctx = ExitStack()
    with ctx:
        def sem(name):
            return ctx.enter_context(nc.semaphore(name))

        def small(name, shape, dt=F32):
            return ctx.enter_context(nc.sbuf_tensor(name, shape, dt))

        arena = ctx.enter_context(nc.sbuf_tensor("arena", [P, O_END], F32))

        def at(off, *dims, rows=P):
            n = 1
            for d in dims:
                n *= d
            v = arena[0:rows, off:off + n]
            if len(dims) == 2:
                v = v.rearrange("p (a b) -> p a b", a=dims[0])
            elif len(dims) == 3:
                v = v.rearrange("p (a b c) -> p a b c", a=dims[0], b=dims[1])
            return v

        bank = [ctx.enter_context(nc.psum_tensor(f"bank{i}", [P, 512], F32)) for i in range(8)]

        slot = [at(O_RING + i * SLOT, SLOT) for i in range(3)] + [at(O_W, SLOT)]
        xT = at(O_XT, KD, S)
        hT = at(O_XT, KD, S)
        xpad = at(O_XPAD, CT, S + 4)
        xdt = at(O_XPAD, 2, T, D)
        ln = at(O_XPAD, 4, D)
        xbc = at(O_XBC, CT, S)
        yT = at(O_XBC, CT, S)
        vext = at(O_V, T, H, DV + 1)
        osig = at(O_V, T, D)
        qT = at(O_QK, H, S)
        kT = at(O_QK + H * S, H, S)
        cb = at(O_QK, G, T, S)
        st = at(O_ST, H, T, S)
        xin = at(O_ST, T, D)
        W = [[at(O_W + (f * NB + b) * 512, 4, P) for b in range(NB)] for f in range(2)]
        oneh = at(O_OH, SH, P, rows=R)
        zs = at(O_Z, T, D)
        xs = at(O_XS, T, D)
        hml = at(O_HML, T, D)
        h = hml
        nrm = at(O_NRM, 2, D)
        col_d = at(O_ROWS, S, rows=R)
        col_o = at(O_ROWS + S, S, rows=R)
        row_t = at(O_ROWS + 2 * S, S, rows=R)
        tmp = [at(O_W + i * S, S, rows=R) for i in range(16)]
        g_z, g_nz, g_u, g_w, g_r, g_s, g_s2, g_p, g_sp, g_dec, g_cum, g_x, g_it, g_m, g_tr, g_zero = tmp
        wgi = at(O_HML, KD, 2, R)
        hh = at(O_Z, T, FE)
        sg = at(O_Z + 2 * KIB, T, FE)
        hhT = at(O_Z + 4 * KIB, 2, S)
        wr = at(O_Z + 6 * KIB, KD, E)
        ytmp = xs
        gate = at(O_QK, T, E + 1)
        score = at(O_QK + 130, T, E)
        choice = at(O_QK + 258, E)
        cand = at(O_QK + 322, E)
        top8 = at(O_QK + 386, EG, 8)
        sel = at(O_QK + 450, 4, E)
        zero64 = at(O_QK + 706, E)

        ident = small("ident", [P, P])
        identb = small("identb", [P, P], BF16)
        negm = small("negm", [P, 2, P], BF16)
        zb = small("zb", [P, P], BF16)
        rc = small("rc", [R, 8])
        convw = small("convw", [P, CT, TAPS])
        convb = small("convb", [P, CT])
        dsk = small("dsk", [P, SH])
        rbias = small("rbias", [P, E])
        ea = small("ea", [R, 1])
        mcol = small("mcol", [R, 1])
        inic = small("inic", [R, 1])
        g0m = small("g0m", [R, 1])
        colT = small("colT", [P, T, R])
        stat = small("stat", [P, 8, 6])
        mv = small("mv", [P, 8, 2])
        vv = small("vv", [P, 5, 16])
        ssq = small("ssq", [P, T, G])
        dcol = small("dcol", [P, 2])
        gsc = small("gsc", [P, 2, EG])
        gt8 = small("gt8", [P, 8])
        need = small("need", [P, 2])

        s_const = sem("s_const")
        s_gatew = sem("s_gatew")
        s_late = sem("s_late")
        s_xin = sem("s_xin")
        s_out = sem("s_out")
        slot_full = [sem(f"slot_full{i}") for i in range(RING2)]
        mix_used = sem("mix_used")
        s_wr = sem("s_wr")
        pads_ready = sem("pads_ready")
        proj_ready = sem("proj_ready")
        gate_read = sem("gate_read")
        proj_evac = sem("proj_evac")
        gates_z = sem("gates_z")
        gates_u = sem("gates_u")
        rows_ready = sem("rows_ready")
        em_arg = sem("em_arg")
        em_ready = sem("em_ready")
        misc_ready = sem("misc_ready")
        misc_evac = sem("misc_evac")
        conv_done = sem("conv_done")
        conv_silu = sem("conv_silu")
        decay_ready = sem("decay_ready")
        decay_exp = sem("decay_exp")
        weight_ready = sem("weight_ready")
        ml_ready = sem("ml_ready")
        ml_read = sem("ml_read")
        xdt_ready = sem("xdt_ready")
        ssm_ready = sem("ssm_ready")
        ssm_read = sem("ssm_read")
        y_gated = sem("y_gated")
        o_sig = sem("o_sig")
        sq_done = sem("sq_done")
        var_ready = sem("var_ready")
        sqrt_done = sem("sqrt_done")
        y_ready = sem("y_ready")
        mix_ready = sem("mix_ready")
        h_ready = sem("h_ready")
        logit_ready = sem("logit_ready")
        score_ready = sem("score_ready")
        gates_done = sem("gates_done")
        gu_ready = sem("gu_ready")
        silu_done = sem("silu_done")
        hh_ready = sem("hh_ready")
        tr_ready = sem("tr_ready")
        hhT_ready = sem("hhT_ready")
        moe_used = sem("moe_used")
        moe_ready = sem("moe_ready")
        out_ready = sem("out_ready")
        s_dve = sem("s_dve")

        loads_in = [len(range(i, LOADS, RING1)) for i in range(RING1)] + [0]

        CPAIR, VSTEP, ZSTEP, OSTEP = 1, 13, 17, 21
        M_COL, M_ST, M_CB, M_XS, M_Y, M_H = 0, 1, 5, 9, 13, 21
        SRC = {(d, t): [b for b, (bd, _, bt, _) in enumerate(BLOCKS) if (bd, bt) == (d, t)]
               for d in range(2) for t in range(T)}

        block = ctx.enter_context(nc.Block())

        @block.sync
        def _(sp):
            def wait_used(m):
                if m < 4:
                    sp.wait_ge(proj_ready, 3 * m + 4)
                elif m < 10:
                    sp.wait_ge(proj_ready, VSTEP + 2 * (m - 4) + 2)
                else:
                    sp.wait_ge(mix_used, m - 9)

            sp.dma_start(wgi, a["wgi"]).then_inc(s_gatew, 16)
            sp.dma_start(xT, a["xT"]).then_inc(s_gatew, 16)
            for n in range(LOADS):
                if n >= RING1:
                    wait_used(n - RING1)
                s = slot[n % RING1]
                if n < 4:
                    src, dst = a["wc"][n], s
                elif n < 10:
                    src, dst = a["wn"][n - 4], s[:, 0:KD * 512]
                else:
                    k0 = 6 * (n - 10)
                    k1 = min(k0 + 6, 2 * KD)
                    src, dst = a["wo"][:, k0 * D:k1 * D], s[:, 0:(k1 - k0) * D]
                sp.dma_start(dst, src).then_inc(slot_full[n % RING1], 16)

            for i in (3, 1, 2, 0):
                if i == 3:
                    sp.wait_ge(ssm_ready, 2 * G)
                else:
                    wait_used(LOADS - RING1 + (i - LOADS) % RING1)
                sp.dma_start(slot[i], a["we"][i]).then_inc(slot_full[i], 16)
            with sp.Fori(0, (ITEMS - 1) // UNROLL - 1) as j:
                for u in range(UNROLL):
                    sp.wait_ge(moe_used, j * UNROLL + (u + 1))
                    sp.dma_start(slot[u], a["we"][bass.ds(j * UNROLL + (RING2 + u), 1)].rearrange(
                        "o p n -> (o p) n")).then_inc(slot_full[u], 16)
            sp.wait_ge(moe_used, ITEMS - RING2)
            sp.dma_start(slot[(ITEMS - 1) % RING2], a["we"][ITEMS - 1]).then_inc(slot_full[(ITEMS - 1) % RING2], 16)

            for t in range(T):
                sp.wait_ge(out_ready, t + 1)
                sp.dma_start(out[0, t * P:(t + 1) * P, :], ytmp[:, t, :]).then_inc(s_out, 16)
            sp.wait_ge(s_out, 16 * T)

        @block.gpsimd
        def _(pool):
            pool.dma_start(rc[:], a["rc"]).then_inc(s_const, 16)
            pool.dma_start(at(O_OH, SH * P, rows=R), a["oneh"]).then_inc(s_const, 16)
            pool.dma_start(ident[:], a["ident"]).then_inc(s_const, 16)
            pool.dma_start(identb[:], a["ident"]).then_inc(s_const, 16)
            pool.dma_start(negm[:], a["negm"]).then_inc(s_const, 16)
            pool.dma_start(convw[:], a["convw"]).then_inc(s_const, 16)
            pool.dma_start(convb[:], a["convb"]).then_inc(s_const, 16)
            pool.dma_start(dsk[:], a["dsk"].to_broadcast([P, SH])).then_inc(s_const, 16)
            pool.dma_start(rbias[:], a["rbias"].to_broadcast([P, E])).then_inc(s_const, 16)
            pool.dma_start(at(O_NRM, 2 * D), a["nrm"].to_broadcast([P, 2 * D])).then_inc(s_const, 16)
            nc.gpsimd.memset(vext[:, :, :, DV:DV + 1], 1.0).then_inc(pads_ready, 1)
            nc.gpsimd.memset(xpad[:, :, 0:2], 0.0).then_inc(pads_ready, 1)
            nc.gpsimd.memset(xpad[:, :, S + 2:S + 4], 0.0).then_inc(pads_ready, 1)
            nc.gpsimd.memset(zb[:], 0.0).then_inc(pads_ready, 1)
            pool.wait_ge(weight_ready, NB)
            pool.dma_start(at(O_ST, T * D), a["x"]).then_inc(s_xin, 16)
            pool.wait_ge(ssm_ready, 2 * G)
            pool.dma_start(at(O_XPAD, 4 * D), a["ln"].to_broadcast([P, 4 * D])).then_inc(s_late, 16)
            pool.wait_ge(y_gated, T)
            pool.dma_start(wr, a["wr"]).then_inc(s_wr, 16)

        @block.tensor
        def _(pe):
            def full(n):
                pe.wait_ge(slot_full[n % RING1], 16 * (n // RING1 + 1))

            def bank_free(n):
                if n == 2:
                    pe.wait_ge(gate_read, 1)
                elif n > 2:
                    pe.wait_ge(proj_evac, n - 2)

            def misc(m):
                if m >= 2:
                    pe.wait_ge(misc_evac, m - 1)
                return bank[4 + m % 2]

            def channels(n):
                bank_free(n)
                for j in range(2):
                    tile = 2 * (n - CPAIR) + j
                    if tile % 6 == 0:
                        full(tile // 6)
                    w = slot[(tile // 6) % RING1].rearrange("p (j k c) -> p j k c", j=6, k=KD)
                    for k in range(KD):
                        mm = nc.tensor.matmul(bank[n % 2][:, j * S:(j + 1) * S], w[:, tile % 6, k, :],
                                              xT[:, k, :], start=(k == 0), stop=(k == KD - 1))
                mm.then_inc(proj_ready, 1)

            def rows(n):
                load, t = 4 + (n - VSTEP) // 2, (n - VSTEP) % 2
                bank_free(n)
                if t == 0:
                    full(load)
                w = slot[load % RING1][:, 0:KD * 512].rearrange("p (k c) -> p k c", c=512)
                for k in range(KD):
                    mm = nc.tensor.matmul(bank[n % 2][:, :], xT[:, k, t * P:(t + 1) * P], w[:, k, :],
                                          start=(k == 0), stop=(k == KD - 1))
                mm.then_inc(proj_ready, 1)

            def decays(fam):
                g = max(fam - 1, 0)
                for b, (d, s, t, diag) in enumerate(BLOCKS):
                    n = fam * NB + b
                    q = ROW0[d if fam == 0 else 2 + d]
                    r = slice(q, q + (H if fam == 0 else SH))
                    ps = bank[2 + n % 2]
                    if n >= 2:
                        pe.wait_ge(weight_ready, n - 1)
                    cols = col_d if diag else col_o
                    for j in range(4):
                        nc.tensor.matmul(ps[:, j * P:(j + 1) * P], oneh[r, 4 * g + j, :],
                                         row_t[r, t * P:(t + 1) * P], start=(j == 0), stop=False,
                                         skip_group_check=True)
                    if diag:
                        nc.tensor.matmul(ps[:, :].rearrange("p (j t) -> p j t", j=4), identb[:],
                                         negm[:, d:d + 1, :].to_broadcast([P, 4, P]), start=False, stop=False,
                                         skip_group_check=True)
                    mm = nc.tensor.matmul(ps[:, :], cols[r, s * P:(s + 1) * P], oneh[r, 4 * g:4 * g + 4, :],
                                          start=False, stop=True, skip_group_check=True)
                    mm.then_inc(decay_ready, 1)

            pe.wait_ge(s_gatew, 32)
            for j in range(2):
                for k in range(KD):
                    mm = nc.tensor.matmul(bank[0][0:R, j * S:(j + 1) * S], wgi[:, k, j, :], xT[:, k, :],
                                          start=(k == 0), stop=(k == KD - 1))
            mm.then_inc(proj_ready, 1)
            for n in range(CPAIR, CPAIR + 4):
                channels(n)
            pe.wait_ge(s_const, 160)
            pe.wait_ge(rows_ready, 1)
            pe.wait_ge(em_ready, 1)
            ps = misc(M_COL)
            for t in range(T):
                mm = nc.tensor.transpose(ps[:, t * P:t * P + R], g_tr[:, t * P:(t + 1) * P], ident[0:R, 0:R])
            mm.then_inc(misc_ready, 1)
            for n in range(CPAIR + 4, CPAIR + 8):
                channels(n)
            pe.wait_ge(proj_evac, 4)
            for hd in range(H):
                ps = misc(M_ST + hd)
                for s in range(T):
                    mm = nc.tensor.matmul(ps[:, s * S:(s + 1) * S], kT[:, hd, s * P:(s + 1) * P], qT[:, hd, :],
                                          start=True, stop=True)
                mm.then_inc(misc_ready, 1)
            for n in range(CPAIR + 8, VSTEP):
                channels(n)
            for n in range(VSTEP, ZSTEP):
                rows(n)
            decays(0)
            for n in range(ZSTEP, OSTEP):
                rows(n)
            pe.wait_ge(pads_ready, 4)
            pe.wait_ge(proj_evac, ZSTEP - 1)
            pe.wait_ge(weight_ready, NB)
            n = 0
            for t in range(T):
                for hd in range(H):
                    for d in range(2):
                        if n >= 2:
                            pe.wait_ge(ml_read, n - 1)
                        for j, b in enumerate(SRC[d, t]):
                            mm = nc.tensor.matmul(bank[6 + n % 2][:, 0:DV + 1], W[0][b][:, hd, :],
                                                  vext[:, BLOCKS[b][1], hd, :], start=(j == 0),
                                                  stop=(j == len(SRC[d, t]) - 1))
                        mm.then_inc(ml_ready, 1)
                        n += 1
            pe.wait_ge(conv_silu, 4)
            for g in range(G):
                ps = misc(M_CB + g)
                for s in range(T):
                    mm = nc.tensor.matmul(ps[:, s * S:(s + 1) * S], xbc[:, g, s * P:(s + 1) * P],
                                          xbc[:, G + g, :], start=True, stop=True)
                mm.then_inc(misc_ready, 1)
            pe.wait_ge(conv_silu, 8)
            for m in range(4):
                ps = misc(M_XS + m)
                t, half = m // 2, m % 2
                for j in range(4):
                    mm = nc.tensor.transpose(ps[:, j * P:(j + 1) * P],
                                             xbc[:, 8 + 4 * half + j, t * P:(t + 1) * P], ident[:])
                mm.then_inc(misc_ready, 1)
            decays(1)
            for g in range(G):
                fam = 1 + g
                if g < G - 1:
                    decays(fam + 1)
                rows(OSTEP + g)
                pe.wait_ge(weight_ready, (fam + 1) * NB)
                pe.wait_ge(xdt_ready, 4)
                for t in range(T):
                    if g == 0:
                        pe.wait_ge(ml_read, 16)
                    else:
                        pe.wait_ge(ssm_read, 2 * (g - 1) + t + 1)
                    for j in range(4):
                        parts = [(d, b) for d in range(2) for b in SRC[d, t]]
                        for i, (d, b) in enumerate(parts):
                            col = (4 * g + j) * HP
                            mm = nc.tensor.matmul(bank[6 + t][:, j * HP:(j + 1) * HP], W[fam % 2][b][:, j, :],
                                                  xdt[:, d, BLOCKS[b][1], col:col + HP], start=(i == 0),
                                                  stop=(i == len(parts) - 1))
                    mm.then_inc(ssm_ready, 1)
            for m in range(8):
                if m % 4 == 0:
                    pe.wait_ge(y_ready, 1 + m // 4)
                ps = misc(M_Y + m)
                for c in range(2):
                    for t in range(T):
                        col = (2 * m + c) % 8 * P
                        mm = nc.tensor.transpose(ps[:, (2 * c + t) * P:(2 * c + t + 1) * P],
                                                 (hml if m < 4 else xs)[:, t, col:col + P], ident[:])
                mm.then_inc(misc_ready, 1)
            pe.wait_ge(proj_evac, OSTEP + 3)
            pe.wait_ge(weight_ready, 5 * NB)
            for n in range(10, LOADS):
                full(n)
                for k in range(6 * (n - 10), min(6 * (n - 10) + 6, 2 * KD)):
                    if k % 2 == 0:
                        pe.wait_ge(misc_evac, M_Y + k // 2 + 1)
                    w = slot[n % RING1].rearrange("p (k c) -> p k c", c=D)
                    for t in range(T):
                        for half in range(2):
                            mm = nc.tensor.matmul(bank[2 * t + half][:, :], yT[:, k, t * P:(t + 1) * P],
                                                  w[:, k - 6 * (n - 10), half * 512:(half + 1) * 512],
                                                  start=(k == 0), stop=(k == 2 * KD - 1))
                mm.then_inc(mix_used, 1)
            pe.wait_ge(h_ready, T)
            for m in range(4):
                ps = misc(M_H + m)
                for c in range(2):
                    for t in range(T):
                        mm = nc.tensor.transpose(ps[:, (2 * c + t) * P:(2 * c + t + 1) * P],
                                                 h[:, t, (2 * m + c) * P:(2 * m + c + 1) * P], ident[:])
                mm.then_inc(misc_ready, 1)
            pe.wait_ge(misc_evac, M_H + 4)
            pe.wait_ge(s_wr, 16)
            for t in range(T):
                for k in range(KD):
                    mm = nc.tensor.matmul(bank[3][:, t * E:(t + 1) * E], hT[:, k, t * P:(t + 1) * P], wr[:, k, :],
                                          start=(k == 0), stop=(k == KD - 1))
            mm.then_inc(logit_ready, 1)
            for i in range(4):
                nc.tensor.matmul(bank[4 + i][:, :], zb[:], zb[:, 0:1].to_broadcast([P, 512]),
                                 start=True, stop=False, skip_group_check=True)

            def moe_full(u, j):
                pe.wait_ge(slot_full[u], (j + (loads_in[u] + 1)) * 16)

            def gate_up(i, u):
                w = slot[u][:, 0:KD * 512].rearrange("p (k c) -> p k c", c=512)
                for t in range(T):
                    if not isinstance(i, int) or i > 0:
                        pe.wait_ge(hh_ready, i * 2 + (t - 1))
                    for k in range(KD):
                        mm = nc.tensor.matmul(bank[t][:, :], hT[:, k, t * P:(t + 1) * P], w[:, k, :],
                                              start=(k == 0), stop=(k == KD - 1))
                    mm.then_inc(gu_ready, 1)

            def down(i, u):
                pe.wait_ge(hh_ready, i * 2 + 2)
                for f in range(2):
                    for t in range(T):
                        mm = nc.tensor.transpose(bank[2][:, (2 * f + t) * P:(2 * f + t + 1) * P],
                                                 hh[:, t, f * P:(f + 1) * P], ident[:])
                mm.then_inc(tr_ready, 1)
                pe.wait_ge(hhT_ready, i + 1)
                w = slot[u][:, KD * 512:].rearrange("p (f c) -> p f c", f=2)
                for f in range(2):
                    for t in range(T):
                        for half in range(2):
                            mm = nc.tensor.matmul(bank[4 + 2 * t + half][:, :], hhT[:, f, t * P:(t + 1) * P],
                                                  w[:, f, half * 512:(half + 1) * 512],
                                                  start=False, stop=False, skip_group_check=True)
                mm.then_inc(moe_used, 1)

            moe_full(0, 0)
            gate_up(0, 0)
            with pe.Fori(0, (ITEMS - 1) // UNROLL) as j:
                for v in range(UNROLL):
                    u = (v + 1) % RING2
                    moe_full(u, j + (v + 1) // RING2)
                    gate_up(j * UNROLL + (v + 1), u)
                    down(j * UNROLL + v, v)
            down(ITEMS - 1, (ITEMS - 1) % RING2)
            for i in range(4):
                mm = nc.tensor.matmul(bank[4 + i][:, :], zb[:], zb[:, 0:1].to_broadcast([P, 512]),
                                      start=False, stop=True, skip_group_check=True)
            mm.then_inc(moe_ready, 1)

        @block.scalar
        def _(act):
            act.wait_ge(s_const, 160)
            act.wait_ge(gates_z, 1)
            nc.scalar.activation(g_u, g_nz, ACT.Exp).then_inc(gates_u, 1)
            nc.scalar.activation(ea[:], rc[:, 2:3], ACT.Exp).then_inc(gates_u, 1)

            def evac(n, dst, src, scale=1.0, func=ACT.Copy):
                act.wait_ge(proj_ready, n + 1)
                nc.scalar.activation(dst, src, func, scale=scale).then_inc(proj_evac, 1)

            def pair(n):
                return bank[n % 2][:, :].rearrange("p (j t) -> p j t", j=2)

            evac(1, qT[:, 0:2, :], pair(1))
            evac(2, qT[:, 2:4, :], pair(2))
            evac(3, kT[:, 0:2, :], pair(3), scale=DQK ** -0.5)
            evac(4, kT[:, 2:4, :], pair(4), scale=DQK ** -0.5)
            act.wait_ge(em_arg, 1)
            nc.scalar.activation(g_tr[0:64, :], g_m[0:64, :], ACT.Exp).then_inc(em_ready, 1)
            act.wait_ge(pads_ready, 4)
            for n in range(CPAIR + 4, VSTEP):
                c = 2 * (n - CPAIR - 4)
                evac(n, xpad[:, c:c + 2, 2:S + 2], pair(n))

            def conv_act(m):
                act.wait_ge(conv_done, 2 * m + 2)
                nc.scalar.activation(xbc[:, 2 * m:2 * m + 2, :], xbc[:, 2 * m:2 * m + 2, :],
                                     ACT.Silu).then_inc(conv_silu, 1)

            def decay_exps(fam):
                for n in range(fam * NB, (fam + 1) * NB):
                    act.wait_ge(decay_ready, n + 1)
                    ps = bank[2 + n % 2]
                    nc.scalar.activation(ps[:, :], ps[:, :], ACT.Exp).then_inc(decay_exp, 1)

            for m in range(4):
                conv_act(m)
            for n in range(VSTEP, ZSTEP):
                blk, t = (n - VSTEP) // 2, (n - VSTEP) % 2
                evac(n, vext[:, t, 2 * blk:2 * blk + 2, 0:DV], pair(n))
            decay_exps(0)
            for n in range(ZSTEP, OSTEP):
                blk, t = (n - ZSTEP) // 2, (n - ZSTEP) % 2
                evac(n, zs[:, t, blk * 512:(blk + 1) * 512], bank[n % 2][:, :], func=ACT.Silu)
            for m in range(4, 8):
                conv_act(m)
            decay_exps(1)
            act.wait_ge(ml_ready, 16)
            for g in range(G):
                if g < G - 1:
                    decay_exps(g + 2)
                n = OSTEP + g
                blk, t = g // 2, g % 2
                evac(n, osig[:, t, blk * 512:(blk + 1) * 512], bank[n % 2][:, :])
            act.wait_ge(proj_evac, OSTEP + 3)
            nc.scalar.activation(at(O_V, T * D), at(O_V, T * D), ACT.Sigmoid).then_inc(o_sig, 1)
            for t in range(T):
                act.wait_ge(y_gated, t + 1)
                for g in range(G):
                    sq = nc.scalar.activation(bank[7][:, 0:256], xs[:, t, g * 256:(g + 1) * 256], ACT.Square,
                                              accum_out=ssq[:, t, g:g + 1])
                    sq.then_inc(sq_done, 1)
                    act.wait_ge(sq_done, t * G + g + 1)
            for i in range(2):
                w = 16 if i == 0 else T
                act.wait_ge(var_ready, i + 1)
                nc.scalar.activation(vv[:, 1, 0:w], vv[:, 0, 0:w], ACT.Sqrt).then_inc(sqrt_done, 1)
            act.wait_ge(logit_ready, 1)
            nc.scalar.activation(score[:, :, :], bank[3][:, 0:T * E].rearrange("p (t e) -> p t e", t=T),
                                 ACT.Sigmoid).then_inc(score_ready, 1)

            def silu_gate(i):
                for t in range(T):
                    act.wait_ge(gu_ready, i * 2 + (t + 1))
                    if not isinstance(i, int) or i > 0:
                        act.wait_ge(hh_ready, i * 2 + (t - 1))
                    nc.scalar.activation(sg[:, t, :], bank[t][:, 0:FE], ACT.Silu).then_inc(silu_done, 1)

            silu_gate(0)
            with act.Fori(1, ITEMS) as i:
                silu_gate(i)
            act.wait_ge(var_ready, 3)
            nc.scalar.activation(vv[:, 1, 0:T], vv[:, 0, 0:T], ACT.Sqrt).then_inc(sqrt_done, 1)

        @block.vector
        def _(dve):
            V = nc.vector
            chain = [0]

            def link(ins):
                ins.then_inc(s_dve, 1)
                chain[0] += 1
                dve.wait_ge(s_dve, chain[0])

            dve.wait_ge(s_const, 160)
            dve.wait_ge(proj_ready, 1)
            link(V.tensor_scalar(g_z, bank[0][0:R, 0:S], rc[:, 0:1], rc[:, 1:2], ALU.add, ALU.mult))
            V.tensor_scalar(g_it, bank[0][0:R, S:2 * S], rc[:, 7:8], None, ALU.add).then_inc(gate_read, 1)
            V.scalar_tensor_tensor(out=g_nz, in0=g_z, scalar=-1.0, in1=g_z, op0=ALU.mult,
                                   op1=ALU.min).then_inc(gates_z, 1)
            link(V.memset(g_zero, 0.0))
            dve.wait_ge(gates_u, 2)
            link(V.tensor_scalar(g_w, g_u, 2.0, None, ALU.add))
            link(V.reciprocal(g_r, g_w))
            link(V.tensor_tensor(g_s, g_u, g_r, ALU.mult))
            link(V.tensor_tensor(g_s2, g_s, g_s, ALU.mult))
            link(V.tensor_scalar(g_p, g_s2, 1.0 / 17.0, None, ALU.mult))
            for k in range(15, 2, -2):
                link(V.scalar_tensor_tensor(out=g_p, in0=g_p, scalar=1.0 / k, in1=g_s2, op0=ALU.add, op1=ALU.mult))
            link(V.scalar_tensor_tensor(out=g_p, in0=g_p, scalar=1.0, in1=g_s, op0=ALU.add, op1=ALU.mult))
            link(V.tensor_scalar(g_w, g_z, 0.0, None, ALU.max))
            link(V.scalar_tensor_tensor(out=g_sp, in0=g_p, scalar=2.0, in1=g_w, op0=ALU.mult, op1=ALU.add))
            link(V.tensor_scalar(mcol[:], ea[:], -1.0, None, ALU.mult))
            link(V.tensor_scalar(g_dec, g_sp, mcol[:], None, ALU.mult))
            link(V.tensor_tensor_scan(g_cum[:, 0:P], g_dec[:, 0:P], g_zero[:, 0:P], 0.0, ALU.add, ALU.add))
            link(V.tensor_tensor(inic[:], g_cum[:, P - 1:P], rc[:, 5:6], ALU.mult))
            link(V.tensor_tensor_scan(g_cum[:, P:S], g_dec[:, P:S], g_zero[:, P:S], inic[:], ALU.add, ALU.add))
            link(V.tensor_scalar(g_x, g_cum, rc[:, 3:4], None, ALU.mult))
            link(V.scalar_tensor_tensor(out=g_x, in0=g_dec, scalar=rc[:, 4:5], in1=g_x, op0=ALU.mult, op1=ALU.add))
            link(V.tensor_tensor(g0m[:], g_cum[:, P - 1:P], rc[:, 6:7], ALU.mult))
            link(V.tensor_tensor(col_d, g_it, g_x, ALU.subtract))
            link(V.tensor_scalar(col_o, col_d, g0m[:], None, ALU.add))
            link(V.memset(g_m[0:64, :], 0.0))
            link(V.tensor_tensor_scan(g_m[0:H, :], col_d[0:H, :], col_d[0:H, :], NEG, ALU.max, ALU.max))
            link(V.tensor_tensor_scan(g_m[32:32 + H, ::-1], col_d[32:32 + H, ::-1], col_d[32:32 + H, ::-1],
                                      NEG, ALU.max, ALU.max))
            link(V.tensor_scalar(row_t[0:64, :], g_m[0:64, :], -1.0, None, ALU.mult))
            link(V.tensor_copy(row_t[64:R, :], g_x[64:R, :]))
            V.tensor_tensor(g_m[0:64, :], row_t[0:64, :], g_x[0:64, :], ALU.subtract).then_inc(em_arg, 1)
            V.tensor_copy(g_tr[64:R, :], g_sp[64:R, :]).then_inc(rows_ready, 1)

            def misc_copy(m, dst, src):
                dve.wait_ge(misc_ready, m + 1)
                V.tensor_copy(dst, src).then_inc(misc_evac, 1)

            def mbank(m, n):
                return bank[4 + m % 2][:, :].rearrange("p (j t) -> p j t", j=n)

            def conv(c):
                link(V.tensor_scalar(xbc[:, c, :], xpad[:, c, 0:S], convw[:, c, 0:1], convb[:, c:c + 1],
                                     ALU.mult, ALU.add))
                for k in range(1, TAPS):
                    ins = V.scalar_tensor_tensor(out=xbc[:, c, :], in0=xpad[:, c, k:k + S],
                                                 scalar=convw[:, c, k:k + 1], in1=xbc[:, c, :],
                                                 op0=ALU.mult, op1=ALU.add)
                    if k < TAPS - 1:
                        link(ins)
                ins.then_inc(conv_done, 1)

            def weights(fam):
                if fam == 2:
                    dve.wait_ge(ml_ready, 16)
                elif fam > 2:
                    dve.wait_ge(ssm_ready, 2 * (fam - 2))
                for b, (d, s, t, _) in enumerate(BLOCKS):
                    n = fam * NB + b
                    dve.wait_ge(decay_exp, n + 1)
                    e = bank[2 + n % 2][:, :].rearrange("p (j t) -> p j t", j=4)
                    if fam == 0:
                        sc = st[:, :, s, t * P:(t + 1) * P]
                    else:
                        sc = cb[:, fam - 1, s:s + 1, t * P:(t + 1) * P].to_broadcast([P, 4, P])
                    V.tensor_tensor(W[fam % 2][b], e, sc, ALU.mult).then_inc(weight_ready, 1)

            misc_copy(M_COL, colT[:], mbank(M_COL, 4)[:, 0:T, 0:R])
            for hd in range(H):
                misc_copy(M_ST + hd, st[:, hd, :, :], mbank(M_ST + hd, 2))
            for c in range(8):
                dve.wait_ge(proj_evac, CPAIR + 4 + c // 2)
                conv(c)
            weights(0)
            for c in range(8, CT):
                dve.wait_ge(proj_evac, CPAIR + 4 + c // 2)
                conv(c)
            n = 0
            for t in range(T):
                for hd in range(H):
                    for d in range(2):
                        ps = bank[6 + n % 2]
                        dst = hml[:, t, hd * DV:(hd + 1) * DV]
                        c = ROW0[d] + hd
                        dve.wait_ge(ml_ready, n + 1)
                        link(V.tensor_scalar(dcol[:, 0:1], ps[:, DV:DV + 1], colT[:, t, c:c + 1], None, ALU.max))
                        link(V.scalar_tensor_tensor(out=dcol[:, 0:1], in0=ps[:, DV:DV + 1], scalar=-1.0,
                                                    in1=dcol[:, 0:1], op0=ALU.mult, op1=ALU.max))
                        link(V.reciprocal(dcol[:, 1:2], dcol[:, 0:1]))
                        if d == 0:
                            ins = V.tensor_scalar(dst, ps[:, 0:DV], dcol[:, 1:2], None, ALU.mult)
                        else:
                            ins = V.scalar_tensor_tensor(out=dst, in0=ps[:, 0:DV], scalar=dcol[:, 1:2], in1=dst,
                                                         op0=ALU.mult, op1=ALU.add)
                        ins.then_inc(ml_read, 1)
                        n += 1
                        dve.wait_ge(ml_read, n)
            for g in range(G):
                misc_copy(M_CB + g, cb[:, g, :, :], mbank(M_CB + g, 2))
            for m in range(4):
                misc_copy(M_XS + m, xs[:, m // 2, (m % 2) * 512:(m % 2 + 1) * 512], bank[4 + (M_XS + m) % 2][:, :])
            dve.wait_ge(misc_evac, M_XS + 4)
            for d in range(2):
                for t in range(T):
                    q = ROW0[2 + d]
                    V.tensor_tensor(xdt[:, d, t, :].rearrange("p (h c) -> p h c", h=SH),
                                    xs[:, t, :].rearrange("p (h c) -> p h c", h=SH),
                                    colT[:, t, q:q + SH].unsqueeze(2).to_broadcast([P, SH, HP]),
                                    ALU.mult).then_inc(xdt_ready, 1)
            dve.wait_ge(xdt_ready, 4)
            for t in range(T):
                v = xs[:, t, :].rearrange("p (h c) -> p h c", h=SH)
                link(V.tensor_tensor(v, v, dsk[:].unsqueeze(2).to_broadcast([P, SH, HP]), ALU.mult))
            weights(1)
            for g in range(G):
                if g < G - 1:
                    weights(g + 2)
                for t in range(T):
                    dve.wait_ge(ssm_ready, 2 * g + t + 1)
                    v = xs[:, t, g * 256:(g + 1) * 256]
                    V.tensor_tensor(v, bank[6 + t][:, 0:256], v, ALU.add).then_inc(ssm_read, 1)
            dve.wait_ge(ssm_read, 2 * G)
            dve.wait_ge(proj_evac, OSTEP - 1)
            for t in range(T):
                V.tensor_tensor(xs[:, t, :], xs[:, t, :], zs[:, t, :], ALU.mult).then_inc(y_gated, 1)

            def rsqrt(w, count):
                link(V.tensor_copy(vv[:, 2, 0:w], vv[:, 0, 0:w]))
                dve.wait_ge(sqrt_done, count)
                link(V.reciprocal(vv[:, 3, 0:w], vv[:, 1, 0:w]))
                link(V.tensor_tensor(vv[:, 4, 0:w], vv[:, 3, 0:w], vv[:, 3, 0:w], ALU.mult))
                link(V.tensor_tensor(vv[:, 4, 0:w], vv[:, 4, 0:w], vv[:, 2, 0:w], ALU.mult))
                link(V.tensor_scalar(vv[:, 4, 0:w], vv[:, 4, 0:w], -0.5, 1.5, ALU.mult, ALU.add))
                link(V.tensor_tensor(vv[:, 3, 0:w], vv[:, 3, 0:w], vv[:, 4, 0:w], ALU.mult))

            for i in range(8):
                ins = V.bn_stats(stat[:, i, :], hml[:, i // H, (i % H) * DV:(i % H + 1) * DV])
            link(ins)
            for i in range(8):
                ins = V.bn_aggr(mv[:, i, :], stat[:, i, :])
            link(ins)
            link(V.tensor_scalar(vv[:, 0, 0:8], mv[:, :, 1], EPS, None, ALU.add))
            dve.wait_ge(sq_done, T * G)
            V.tensor_scalar(vv[:, 0, 8:16], ssq[:].rearrange("p t g -> p (t g)"), 1.0 / 256, EPS, ALU.mult,
                            ALU.add).then_inc(var_ready, 1)
            dve.wait_ge(var_ready, 1)
            rsqrt(16, 1)
            for i in range(8):
                v = hml[:, i // H, (i % H) * DV:(i % H + 1) * DV]
                ins = V.tensor_scalar(v, v, mv[:, i, 0:1], vv[:, 3, i:i + 1], ALU.subtract, ALU.mult)
            link(ins)
            dve.wait_ge(o_sig, 1)
            for t in range(T):
                link(V.tensor_tensor(hml[:, t, :], hml[:, t, :], nrm[:, 0, :], ALU.mult))
                ins = V.tensor_tensor(hml[:, t, :], hml[:, t, :], osig[:, t, :], ALU.mult)
                if t == 0:
                    link(ins)
            ins.then_inc(y_ready, 1)
            for i in range(8):
                v = xs[:, i // G, (i % G) * 256:(i % G + 1) * 256]
                n = nrm[:, 1, (i % G) * 256:(i % G + 1) * 256]
                ins = V.scalar_tensor_tensor(out=v, in0=v, scalar=vv[:, 3, 8 + i:9 + i], in1=n,
                                             op0=ALU.mult, op1=ALU.mult)
            ins.then_inc(y_ready, 1)
            for m in range(8):
                misc_copy(M_Y + m, yT[:, 2 * m:2 * m + 2, :], mbank(M_Y + m, 2))

            def layer_norm(src, dst, which, count, signal, first_bank):
                for t in range(T):
                    for half in range(2):
                        c = slice(half * 512, (half + 1) * 512)
                        link(V.scalar_tensor_tensor(out=dst[:, t, c], in0=src[:, t, c], scalar=ALPHA,
                                                    in1=bank[first_bank + 2 * t + half][:, :],
                                                    op0=ALU.mult, op1=ALU.add))
                        link(V.bn_stats(stat[:, 2 * t + half, :], dst[:, t, c]))
                    link(V.bn_aggr(mv[:, t, :], stat[:, 2 * t:2 * t + 2, :].rearrange("p a b -> p (a b)")))
                V.tensor_scalar(vv[:, 0, 0:T], mv[:, 0:T, 1], EPS, None, ALU.add).then_inc(var_ready, 1)
                dve.wait_ge(var_ready, count)
                rsqrt(T, count)
                for t in range(T):
                    v = dst[:, t, :]
                    link(V.tensor_scalar(v, v, mv[:, t, 0:1], vv[:, 3, t:t + 1], ALU.subtract, ALU.mult))
                    link(V.tensor_tensor(v, v, ln[:, 2 * which, :], ALU.mult))
                    V.tensor_tensor(v, v, ln[:, 2 * which + 1, :], ALU.add).then_inc(signal, 1)
                dve.wait_ge(signal, T)

            dve.wait_ge(mix_used, 3)
            dve.wait_ge(s_xin, 16)
            dve.wait_ge(s_late, 16)
            layer_norm(xin, h, 0, 2, h_ready, 0)
            for m in range(4):
                misc_copy(M_H + m, hT[:, 2 * m:2 * m + 2, :], mbank(M_H + m, 2))

            def top_k(dst, vals, thr, k, w):
                link(V.tensor_scalar(sel[:, 0, 0:w], vals, thr, None, ALU.is_gt, ALU.add, accum_out=need[:, 0:1]))
                link(V.tensor_scalar(need[:, 1:2], need[:, 0:1], -1.0, float(k), ALU.mult, ALU.add))
                link(V.tensor_scalar(sel[:, 1, 0:w], vals, thr, None, ALU.is_equal))
                link(V.tensor_tensor_scan(sel[:, 2, 0:w], sel[:, 1, 0:w], zero64[:, 0:w], 0.0, ALU.add, ALU.add))
                link(V.scalar_tensor_tensor(out=sel[:, 1, 0:w], in0=sel[:, 2, 0:w], scalar=need[:, 1:2],
                                            in1=sel[:, 1, 0:w], op0=ALU.is_le, op1=ALU.mult))
                link(V.tensor_tensor(dst, sel[:, 0, 0:w], sel[:, 1, 0:w], ALU.add))

            link(V.memset(zero64, 0.0))
            link(V.memset(gate[:, :, 0:1], 1.0))
            dve.wait_ge(score_ready, 1)
            for t in range(T):
                link(V.tensor_tensor(choice, score[:, t, :], rbias[:], ALU.add))
                for g in range(EG):
                    ins = V.max(top8[:, g, :], choice[:, g * 8:(g + 1) * 8])
                link(ins)
                link(V.tensor_tensor(gsc[:, 0, :], top8[:, :, 0], top8[:, :, 1], ALU.add))
                link(V.max(gt8[:], gsc[:, 0, :]))
                top_k(gsc[:, 1, :], gsc[:, 0, :], gt8[:, TOPG - 1:TOPG], TOPG, EG)
                gm = gsc[:, 1, :].unsqueeze(2).to_broadcast([P, EG, 8])
                c3 = cand.rearrange("p (g e) -> p g e", g=EG)
                link(V.tensor_tensor(c3, choice.rearrange("p (g e) -> p g e", g=EG), gm, ALU.mult))
                link(V.tensor_scalar(gsc[:, 0, :], gsc[:, 1, :], BIG, -BIG, ALU.mult, ALU.add))
                link(V.tensor_tensor(c3, c3, gsc[:, 0, :].unsqueeze(2).to_broadcast([P, EG, 8]), ALU.add))
                link(V.max(gt8[:], cand))
                top_k(sel[:, 3, :], cand, gt8[:, TOPK - 1:TOPK], TOPK, E)
                link(V.tensor_tensor(cand, sel[:, 3, :], score[:, t, :], ALU.mult))
                link(V.tensor_reduce(need[:, 0:1], cand, AX_X, ALU.add))
                link(V.reciprocal(need[:, 1:2], need[:, 0:1]))
                V.tensor_scalar(gate[:, t, 1:E + 1], cand, need[:, 1:2], ROUTED_SCALE, ALU.mult,
                                ALU.mult).then_inc(gates_done, 1)
                dve.wait_ge(gates_done, t + 1)

            def hidden(i):
                for t in range(T):
                    dve.wait_ge(silu_done, i * 2 + (t + 1))
                    if t == 0 and (not isinstance(i, int) or i > 0):
                        dve.wait_ge(tr_ready, i)
                    col = gate[:, t, i:i + 1] if isinstance(i, int) else gate[:, t, bass.ds(i, 1)]
                    V.scalar_tensor_tensor(out=hh[:, t, :], in0=sg[:, t, :], scalar=col,
                                           in1=bank[t][:, FE:2 * FE], op0=ALU.mult,
                                           op1=ALU.mult).then_inc(hh_ready, 1)

            def hidden_t(i):
                dve.wait_ge(tr_ready, i + 1)
                if not isinstance(i, int) or i > 0:
                    dve.wait_ge(moe_used, i)
                V.tensor_copy(hhT[:], bank[2][:, :].rearrange("p (f t) -> p f t", f=2)).then_inc(hhT_ready, 1)

            hidden(0)
            hidden_t(0)
            with dve.Fori(1, ITEMS) as i:
                hidden(i)
                hidden_t(i)
            dve.wait_ge(moe_ready, 1)
            layer_norm(h, ytmp, 1, 3, out_ready, 4)


NAMES = ["wgi", "xT", "wc", "wn", "wo", "we", "rc", "oneh", "ident", "negm", "convw", "convb", "dsk", "rbias",
         "nrm", "ln", "x", "wr"]


def layout(**v):
    import numpy as np

    f = np.float32
    v = {k: np.asarray(x) for k, x in v.items()}
    x = v["x"][0]
    w = v["w_in"][0]
    q0, k0, v0, o0, i0, f0, z0, c0, d0 = 0, 512, 1024, 2048, 3072, 3080, 3088, 4112, 6160
    rows = lambda m: m.reshape(-1, P, m.shape[1]).transpose(1, 0, 2)
    out = {}
    out["x"] = rows(x).reshape(P, T * D)
    out["xT"] = rows(x.T)
    wgi = np.zeros((D, 2, R), f)
    for d in range(2):
        wgi[:, 0, ROW0[d]:ROW0[d] + H] = w[:, f0 + d * H:f0 + (d + 1) * H]
        wgi[:, 1, ROW0[d]:ROW0[d] + H] = w[:, i0 + d * H:i0 + (d + 1) * H]
        wgi[:, 0, ROW0[2 + d]:ROW0[2 + d] + SH] = w[:, d0 + d * SH:d0 + (d + 1) * SH]
    out["wgi"] = wgi.reshape(KD, P, 2, R).transpose(1, 0, 2, 3)
    rc = np.zeros((R, 8), f)
    rc[0:64, 1] = -1
    rc[64:, 1] = 1
    rc[:, 2] = NEG
    rc[:, 3] = 1
    rc[0:64, 5] = 1
    rc[64:, 6] = 1
    for d in range(2):
        m, s = slice(ROW0[d], ROW0[d] + H), slice(ROW0[2 + d], ROW0[2 + d] + SH)
        rc[m, 0] = v["ml_f_bias"][0, d * H:(d + 1) * H]
        rc[m, 2] = 0
        rc[m, 7] = v["ml_i_bias"][0, d * H:(d + 1) * H]
        rc[s, 0] = v["dt_bias"][0, d * SH:(d + 1) * SH]
        rc[s, 2] = v["a_log"][0, d * SH:(d + 1) * SH]
        if d == 1:
            rc[m, 3] = rc[s, 3] = -1
            rc[m, 4] = rc[s, 4] = 1
    out["rc"] = rc
    xbc_order = np.concatenate([np.arange(D, CH), np.arange(D)])
    chans = np.concatenate([np.arange(q0, v0), c0 + xbc_order])
    wc = w[:, chans].reshape(KD, P, 4, 6, P)
    out["wc"] = wc.transpose(2, 1, 3, 0, 4).reshape(4, P, SLOT)
    wn = np.concatenate([w[:, v0:o0], w[:, z0:c0], w[:, o0:i0]], 1).reshape(KD, P, 6, 512)
    out["wn"] = wn.transpose(2, 1, 0, 3).reshape(6, P, KD * 512)
    out["wo"] = rows(v["w_out"][0]).reshape(P, 2 * KD * D)
    gate = np.concatenate([v["w_sh_gate"], v["w_exp_gate"][0]], 0).reshape(ITEMS, KD, P, 1, FE)
    up = np.concatenate([v["w_sh_up"], v["w_exp_up"][0]], 0).reshape(ITEMS, KD, P, 1, FE)
    gu = np.concatenate([gate, up], 3).transpose(0, 2, 1, 3, 4).reshape(ITEMS, P, KD * 512)
    dn = np.concatenate([v["w_sh_down"], v["w_exp_down"][0]], 0).reshape(ITEMS, 2, P, D)
    out["we"] = np.concatenate([gu, dn.transpose(0, 2, 1, 3).reshape(ITEMS, P, 2 * D)], 2)
    oneh = np.zeros((R, SH, P), f)
    for q in ROW0:
        for r in range(min(SH, R - q)):
            oneh[q + r, r, :] = 1
    out["oneh"] = oneh.reshape(R, SH * P)
    out["ident"] = np.eye(P, dtype=f)
    s, t = np.arange(P)[:, None], np.arange(P)[None, :]
    out["negm"] = np.stack([np.where(s <= t, 0, NEG), np.where(s >= t, 0, NEG)], 1).astype(f)
    out["convw"] = v["conv_w"][0][:, xbc_order].reshape(TAPS, CT, P).transpose(2, 1, 0)
    out["convb"] = v["conv_b"][0][xbc_order].reshape(CT, P).T
    out["dsk"] = v["d_skip"]
    out["rbias"] = v["router_bias"]
    out["nrm"] = np.concatenate([v["ml_norm_w"], v["ssm_norm_w"]], 1)
    out["ln"] = np.concatenate([v["ln1_g"], v["ln1_b"], v["ln2_g"], v["ln2_b"]], 1)
    out["wr"] = rows(v["w_router"][0])
    return {n: np.ascontiguousarray(out[n]) for n in NAMES}


def kernel(**inputs):
    import concourse.bacc as _bacc
    from concourse import mybir as _mybir
    from concourse.bass_utils import run_bass_kernel_spmd as _run

    nc = _bacc.Bacc("TRN2", target_bir_lowering=False, num_devices=1)
    arrays, args = {}, {}
    for name, arr in layout(**inputs).items():
        arrays[f"in_{name}_dram"] = arr
        args[name] = nc.dram_tensor(f"in_{name}_dram", arr.shape, _mybir.dt.from_np(arr.dtype),
                                    kind="ExternalInput").ap()
    out = nc.dram_tensor("out_0_dram", (1, S, D), _mybir.dt.float32, kind="ExternalOutput").ap()
    build(nc, args, out)
    r = _run(nc, [arrays], core_ids=[0])
    return r.results[0]["out_0_dram"]
```

```python
from contextlib import ExitStack

import concourse.bass as bass
from concourse import mybir

F32 = mybir.dt.float32
F32R = mybir.dt.float32r
BF16 = mybir.dt.bfloat16
I32 = mybir.dt.int32
ALU = mybir.AluOpType
ACT = mybir.ActivationFunctionType
AX_X = mybir.AxisListType.X

P = 128
D = 1024
S = 256
T = S // P
KD = D // P
H = 4
DV = D // H
DQK = DV // 2
SH = 16
G = 4
HP = 64
NST = 128
CH = D + 2 * G * NST
CT = CH // P
TAPS = 5
E = 64
EG = 8
TOPG = 4
TOPK = 8
FE = D // 4
ROUTED_SCALE = 2.5
EPS = 1e-5
ALPHA = 2 ** 0.25
R = 112
ROW0 = (0, 32, 64, 96)
NEG = -1.0e30
BIG = 1.0e30

KIB = 256
SLOT = 24 * KIB
O_RING = 0
O_XT = 72 * KIB
O_XPAD = 80 * KIB
O_XBC = O_XPAD + CT * (S + 4)
O_V = O_XBC + CT * S
O_QK = O_V + T * H * (DV + 1)
O_ST = O_QK + 8 * KIB
O_W = O_ST + 8 * KIB
O_OH = O_W + 24 * KIB
O_Z = O_OH + 8 * KIB
O_XS = O_Z + 8 * KIB
O_HML = O_XS + 8 * KIB
O_NRM = O_HML + 8 * KIB
O_ROWS = O_NRM + 8 * KIB
O_END = O_ROWS + 3 * KIB

BLOCKS = [(0, 0, 0, True), (0, 0, 1, False), (0, 1, 1, True),
          (1, 0, 0, True), (1, 1, 0, False), (1, 1, 1, True)]
NB = len(BLOCKS)
LOADS = 14
RING1 = 3
PAIR_SLOTS = ((3, 2), (0, 1))
PAIRS = E // 2
M = P // 2
PASSES = S // M
RKW = PASSES * E + 4


def build(nc, a, out):
    ctx = ExitStack()
    with ctx:
        def sem(name):
            return ctx.enter_context(nc.semaphore(name))

        def small(name, shape, dt=F32):
            return ctx.enter_context(nc.sbuf_tensor(name, shape, dt))

        arena = ctx.enter_context(nc.sbuf_tensor("arena", [P, O_END], F32))
        arena_at = nc.sbuf_base - 4 * O_END

        def rounded(name, off, *dims):
            assert arena_at % 32 == 0
            return nc.alloc_sbuf_tensor_at(name, [P, *dims], F32R, offset=arena_at + 4 * off)

        def at(off, *dims, rows=P):
            n = 1
            for d in dims:
                n *= d
            v = arena[0:rows, off:off + n]
            if len(dims) == 2:
                v = v.rearrange("p (a b) -> p a b", a=dims[0])
            elif len(dims) == 3:
                v = v.rearrange("p (a b c) -> p a b c", a=dims[0], b=dims[1])
            return v

        bank = [ctx.enter_context(nc.psum_tensor(f"bank{i}", [P, 512], F32)) for i in range(8)]

        slot = [at(O_RING + i * SLOT, SLOT) for i in range(3)] + [at(O_W, SLOT)]
        xT = at(O_XT, KD, S)
        hT = at(O_XT, KD, S)
        xpad = at(O_XPAD, CT, S + 4)
        xdt = at(O_XPAD, 2, T, D)
        ln = at(O_XPAD, 4, D)
        xbc = at(O_XBC, CT, S)
        yT = at(O_XBC, CT, S)
        vext = at(O_V, T, H, DV + 1)
        osig = at(O_V, T, D)
        qT = at(O_QK, H, S)
        kT = at(O_QK + H * S, H, S)
        cb = at(O_QK, G, T, S)
        st = at(O_ST, H, T, S)
        xin = at(O_ST, T, D)
        W = [[at(O_W + (f * NB + b) * 512, 4, P) for b in range(NB)] for f in range(2)]
        oneh = at(O_OH, SH, P, rows=R)
        zs = at(O_Z, T, D)
        xs = at(O_XS, T, D)
        hml = at(O_HML, T, D)
        h = hml
        nrm = at(O_NRM, 2, D)
        col_d = at(O_ROWS, S, rows=R)
        col_o = at(O_ROWS + S, S, rows=R)
        row_t = at(O_ROWS + 2 * S, S, rows=R)
        tmp = [at(O_W + i * S, S, rows=R) for i in range(16)]
        g_z, g_nz, g_u, g_w, g_r, g_s, g_s2, g_p, g_sp, g_dec, g_cum, g_x, g_it, g_m, g_tr, g_zero = tmp
        wgi = at(O_HML, KD, 2, R)
        convw = at(O_HML + KD * 2 * R, CT, TAPS)
        hh = at(O_OH, T, FE)
        sg = at(O_OH + 2 * KIB, T, FE)
        hhT = at(O_OH + 4 * KIB, 2, S)
        wr = at(O_OH + 6 * KIB, KD, E)
        ytmp = xs
        gate = at(O_QK, T, PASSES * E)
        rk = at(O_QK + 512, T, RKW)
        o_rt = O_QK + 512 + T * RKW
        score = at(o_rt, T, E)
        choice = at(o_rt + 128, E)
        cand = at(o_rt + 192, E)
        top8 = at(o_rt + 256, EG, 8)
        sel = at(o_rt + 320, 4, E)
        zero64 = at(o_rt + 576, E)
        h_part = [nc.alloc_sbuf_tensor_at(f"h_part{i}", [P, T, D], BF16,
                                          offset=arena_at + 4 * (O_XBC + i * T * D // 2)) for i in range(3)]
        h_rest = xs
        onehotb = [nc.alloc_sbuf_tensor_at(f"onehotb{i}", [P, T, 2 * M], BF16,
                                           offset=arena_at + 4 * (O_XBC + 3 * T * D // 2 + i * T * M))
                   for i in range(2)]
        onehot = [at(O_Z + i * 256, T, 2 * M) for i in range(2)]
        onehotT = [rounded(f"onehotT{i}", O_Z + 512 + i * 256, T, P) for i in range(2)]
        psg = at(O_Z + 1024, FE)
        phh = at(O_Z + 1280, FE)
        phhT = at(O_Z + 1536, 2, P)
        iota = at(O_Z + 1792, M)
        gcol = at(O_Z + 1856, 1)
        hc = [at(O_V + i * KD * P, KD, P) for i in range(2)]
        y_hi = rounded("y_hi", O_ST, D)
        y_lo = rounded("y_lo", O_ST + D, D)

        ident = small("ident", [P, P])
        identb = small("identb", [P, P], BF16)
        negm = small("negm", [P, 2, P], BF16)
        zb = small("zb", [P, P], BF16)
        rc = small("rc", [R, 8])
        convb = small("convb", [P, CT])
        dsk = small("dsk", [P, SH])
        rbias = small("rbias", [P, E])
        ea = small("ea", [R, 1])
        mcol = small("mcol", [R, 1])
        inic = small("inic", [R, 1])
        g0m = small("g0m", [R, 1])
        colT = small("colT", [P, T, R])
        stat = small("stat", [P, 8, 6])
        mv = small("mv", [P, 8, 2])
        vv = small("vv", [P, 5, 16])
        ssq = small("ssq", [P, T, G])
        dcol = small("dcol", [P, 2])
        gsc = small("gsc", [P, 2, EG])
        gt8 = small("gt8", [P, 8])
        selb = small("selb", [P, T, E], BF16)
        before = small("before", [P, P], BF16)
        onesb = small("onesb", [P, P], BF16)
        rounds_f = small("rounds_f", [P, 2])
        rounds = small("rounds", [1, 1], I32)
        need = small("need", [P, 2])

        s_const = sem("s_const")
        s_gatew = sem("s_gatew")
        s_late = sem("s_late")
        s_xin = sem("s_xin")
        s_out = sem("s_out")
        slot_full = [sem(f"slot_full{i}") for i in range(RING1 + 1)]
        mix_used = sem("mix_used")
        s_wr = sem("s_wr")
        pads_ready = sem("pads_ready")
        proj_ready = sem("proj_ready")
        gate_read = sem("gate_read")
        proj_evac = sem("proj_evac")
        gates_z = sem("gates_z")
        gates_u = sem("gates_u")
        rows_ready = sem("rows_ready")
        em_arg = sem("em_arg")
        em_ready = sem("em_ready")
        misc_ready = sem("misc_ready")
        misc_evac = sem("misc_evac")
        conv_done = sem("conv_done")
        conv_silu = sem("conv_silu")
        decay_ready = sem("decay_ready")
        decay_exp = sem("decay_exp")
        weight_ready = sem("weight_ready")
        ml_ready = sem("ml_ready")
        ml_read = sem("ml_read")
        xdt_ready = sem("xdt_ready")
        ssm_ready = sem("ssm_ready")
        ssm_read = sem("ssm_read")
        y_gated = sem("y_gated")
        o_sig = sem("o_sig")
        sq_done = sem("sq_done")
        var_ready = sem("var_ready")
        sqrt_done = sem("sqrt_done")
        y_ready = sem("y_ready")
        mix_ready = sem("mix_ready")
        h_ready = sem("h_ready")
        logit_ready = sem("logit_ready")
        score_ready = sem("score_ready")
        gates_done = sem("gates_done")
        h_split = sem("h_split")
        sh_gu = sem("sh_gu")
        sh_silu = sem("sh_silu")
        sh_hh = sem("sh_hh")
        sh_tr = sem("sh_tr")
        sh_hhT = sem("sh_hhT")
        sh_used = sem("sh_used")
        sel_bf = sem("sel_bf")
        rank_ready = sem("rank_ready")
        rounds_ready = sem("rounds_ready")
        iota_ready = sem("iota_ready")
        empty_ready = sem("empty_ready")
        onehot_made = sem("onehot_made")
        onehot_ready = sem("onehot_ready")
        gather_ready = sem("gather_ready")
        gathered = sem("gathered")
        slotT_ready = sem("slotT_ready")
        slotT_read = sem("slotT_read")
        gu_ready = sem("gu_ready")
        silu_done = sem("silu_done")
        hidden_ready = sem("hidden_ready")
        hidT_ready = sem("hidT_ready")
        hidT_read = sem("hidT_read")
        down_ready = sem("down_ready")
        yhi_ready = sem("yhi_ready")
        ylo_ready = sem("ylo_ready")
        moe_ready = sem("moe_ready")
        out_ready = sem("out_ready")
        s_dve = sem("s_dve")

        loads_in = [len(range(i, LOADS, RING1)) for i in range(RING1)] + [0]

        CPAIR, VSTEP, ZSTEP, OSTEP = 1, 13, 17, 21
        M_COL, M_ST, M_CB, M_XS, M_Y, M_H = 0, 1, 5, 9, 13, 21
        SRC = {(d, t): [b for b, (bd, _, bt, _) in enumerate(BLOCKS) if (bd, bt) == (d, t)]
               for d in range(2) for t in range(T)}

        block = ctx.enter_context(nc.Block())

        @block.sync
        def _(sp):
            def wait_used(m):
                if m < 4:
                    sp.wait_ge(proj_ready, 3 * m + 4)
                elif m < 10:
                    sp.wait_ge(proj_ready, VSTEP + 2 * (m - 4) + 2)
                elif m < 13:
                    sp.wait_ge(mix_used, m - 9)
                else:
                    sp.wait_ge(sh_used, 1)

            sp.dma_start(wgi, a["wgi"]).then_inc(s_gatew, 16)
            sp.dma_start(xT, a["xT"]).then_inc(s_gatew, 16)
            for n in range(LOADS):
                if n >= RING1:
                    wait_used(n - RING1)
                s = slot[n % RING1]
                if n < 4:
                    src, dst = a["wc"][n], s
                elif n < 10:
                    src, dst = a["wn"][n - 4], s[:, 0:KD * 512]
                elif n == 13:
                    src, dst = a["ws"], s
                else:
                    k0 = 6 * (n - 10)
                    k1 = min(k0 + 6, 2 * KD)
                    src, dst = a["wo"][:, k0 * D:k1 * D], s[:, 0:(k1 - k0) * D]
                sp.dma_start(dst, src).then_inc(slot_full[n % RING1], 16)

            for e, (s, m) in enumerate(((3, None), (2, 11), (0, 12), (1, 13))):
                if m is None:
                    sp.wait_ge(ssm_ready, 2 * G)
                else:
                    wait_used(m)
                sp.dma_start(slot[s], a["we"][e]).then_inc(slot_full[s], 16)
            sp.wait_ge(rounds_ready, 1)
            n_rounds = sp.value_load(rounds[0:1, 0:1], min_val=PAIRS // 2, max_val=PASSES * PAIRS // 2)
            with sp.Fori(1, n_rounds) as j:
                for v in range(2):
                    for e in range(2):
                        if e == 0:
                            sp.wait_ge(down_ready, j * 4 + (2 * v - 2))
                        s = PAIR_SLOTS[v][e]
                        sp.dma_start(slot[s], a["we"][bass.ds((j * 4 + (2 * v + e)) % E, 1)].rearrange(
                            "o p n -> (o p) n")).then_inc(slot_full[s], 16)

            for t in range(T):
                sp.wait_ge(out_ready, t + 1)
                sp.dma_start(out[0, t * P:(t + 1) * P, :], ytmp[:, t, :]).then_inc(s_out, 16)
            sp.wait_ge(s_out, 16 * T)

        @block.gpsimd
        def _(pool):
            pool.dma_start(rc[:], a["rc"]).then_inc(s_const, 16)
            pool.dma_start(at(O_OH, SH * P, rows=R), a["oneh"]).then_inc(s_const, 16)
            pool.dma_start(ident[:], a["ident"]).then_inc(s_const, 16)
            pool.dma_start(identb[:], a["ident"]).then_inc(s_const, 16)
            pool.dma_start(negm[:], a["negm"]).then_inc(s_const, 16)
            pool.dma_start(at(O_HML + KD * 2 * R, CT * TAPS), a["convw"]).then_inc(s_const, 16)
            pool.dma_start(convb[:], a["convb"]).then_inc(s_const, 16)
            pool.dma_start(dsk[:], a["dsk"].to_broadcast([P, SH])).then_inc(s_const, 16)
            pool.dma_start(rbias[:], a["rbias"].to_broadcast([P, E])).then_inc(s_const, 16)
            pool.dma_start(at(O_NRM, 2 * D), a["nrm"].to_broadcast([P, 2 * D])).then_inc(s_const, 16)
            nc.gpsimd.memset(vext[:, :, :, DV:DV + 1], 1.0).then_inc(pads_ready, 1)
            nc.gpsimd.memset(xpad[:, :, 0:2], 0.0).then_inc(pads_ready, 1)
            nc.gpsimd.memset(xpad[:, :, S + 2:S + 4], 0.0).then_inc(pads_ready, 1)
            nc.gpsimd.memset(zb[:], 0.0).then_inc(pads_ready, 1)
            nc.gpsimd.memset(onesb[:], 1.0).then_inc(pads_ready, 1)
            pool.dma_start(before[:], a["before"]).then_inc(s_const, 16)
            pool.wait_ge(weight_ready, NB)
            pool.dma_start(at(O_ST, T * D), a["x"]).then_inc(s_xin, 16)
            pool.wait_ge(ssm_ready, 2 * G)
            pool.dma_start(at(O_XPAD, 4 * D), a["ln"].to_broadcast([P, 4 * D])).then_inc(s_late, 16)
            pool.wait_ge(y_gated, T)
            pool.dma_start(wr, a["wr"]).then_inc(s_wr, 16)
            nc.gpsimd.iota(iota, [[1, M]], base=0, channel_multiplier=0,
                           allow_small_or_imprecise_dtypes=True).then_inc(iota_ready, 1)

        @block.tensor
        def _(pe):
            def full(n):
                pe.wait_ge(slot_full[n % RING1], 16 * (n // RING1 + 1))

            def bank_free(n):
                if n == 2:
                    pe.wait_ge(gate_read, 1)
                elif n > 2:
                    pe.wait_ge(proj_evac, n - 2)

            def misc(m):
                if m >= 2:
                    pe.wait_ge(misc_evac, m - 1)
                return bank[4 + m % 2]

            def channels(n):
                bank_free(n)
                for j in range(2):
                    tile = 2 * (n - CPAIR) + j
                    if tile % 6 == 0:
                        full(tile // 6)
                    w = slot[(tile // 6) % RING1].rearrange("p (j k c) -> p j k c", j=6, k=KD)
                    for k in range(KD):
                        mm = nc.tensor.matmul(bank[n % 2][:, j * S:(j + 1) * S], w[:, tile % 6, k, :],
                                              xT[:, k, :], start=(k == 0), stop=(k == KD - 1))
                mm.then_inc(proj_ready, 1)

            def rows(n):
                load, t = 4 + (n - VSTEP) // 2, (n - VSTEP) % 2
                bank_free(n)
                if t == 0:
                    full(load)
                w = slot[load % RING1][:, 0:KD * 512].rearrange("p (k c) -> p k c", c=512)
                for k in range(KD):
                    mm = nc.tensor.matmul(bank[n % 2][:, :], xT[:, k, t * P:(t + 1) * P], w[:, k, :],
                                          start=(k == 0), stop=(k == KD - 1))
                mm.then_inc(proj_ready, 1)

            def decays(fam):
                g = max(fam - 1, 0)
                for b, (d, s, t, diag) in enumerate(BLOCKS):
                    n = fam * NB + b
                    q = ROW0[d if fam == 0 else 2 + d]
                    r = slice(q, q + (H if fam == 0 else SH))
                    ps = bank[2 + n % 2]
                    if n >= 2:
                        pe.wait_ge(weight_ready, n - 1)
                    cols = col_d if diag else col_o
                    for j in range(4):
                        nc.tensor.matmul(ps[:, j * P:(j + 1) * P], oneh[r, 4 * g + j, :],
                                         row_t[r, t * P:(t + 1) * P], start=(j == 0), stop=False,
                                         skip_group_check=True)
                    if diag:
                        nc.tensor.matmul(ps[:, :].rearrange("p (j t) -> p j t", j=4), identb[:],
                                         negm[:, d:d + 1, :].to_broadcast([P, 4, P]), start=False, stop=False,
                                         skip_group_check=True)
                    mm = nc.tensor.matmul(ps[:, :], cols[r, s * P:(s + 1) * P], oneh[r, 4 * g:4 * g + 4, :],
                                          start=False, stop=True, skip_group_check=True)
                    mm.then_inc(decay_ready, 1)

            pe.wait_ge(s_gatew, 32)
            for j in range(2):
                for k in range(KD):
                    mm = nc.tensor.matmul(bank[0][0:R, j * S:(j + 1) * S], wgi[:, k, j, :], xT[:, k, :],
                                          start=(k == 0), stop=(k == KD - 1))
            mm.then_inc(proj_ready, 1)
            for n in range(CPAIR, CPAIR + 4):
                channels(n)
            pe.wait_ge(s_const, 176)
            pe.wait_ge(rows_ready, 1)
            pe.wait_ge(em_ready, 1)
            ps = misc(M_COL)
            for t in range(T):
                mm = nc.tensor.transpose(ps[:, t * P:t * P + R], g_tr[:, t * P:(t + 1) * P], ident[0:R, 0:R])
            mm.then_inc(misc_ready, 1)
            for n in range(CPAIR + 4, CPAIR + 8):
                channels(n)
            pe.wait_ge(proj_evac, 4)
            for hd in range(H):
                ps = misc(M_ST + hd)
                for s in range(T):
                    mm = nc.tensor.matmul(ps[:, s * S:(s + 1) * S], kT[:, hd, s * P:(s + 1) * P], qT[:, hd, :],
                                          start=True, stop=True)
                mm.then_inc(misc_ready, 1)
            for n in range(CPAIR + 8, VSTEP):
                channels(n)
            for n in range(VSTEP, ZSTEP):
                rows(n)
            decays(0)
            for n in range(ZSTEP, OSTEP):
                rows(n)
            pe.wait_ge(pads_ready, 5)
            pe.wait_ge(proj_evac, ZSTEP - 1)
            pe.wait_ge(weight_ready, NB)
            n = 0
            for t in range(T):
                for hd in range(H):
                    for d in range(2):
                        if n >= 2:
                            pe.wait_ge(ml_read, n - 1)
                        for j, b in enumerate(SRC[d, t]):
                            mm = nc.tensor.matmul(bank[6 + n % 2][:, 0:DV + 1], W[0][b][:, hd, :],
                                                  vext[:, BLOCKS[b][1], hd, :], start=(j == 0),
                                                  stop=(j == len(SRC[d, t]) - 1))
                        mm.then_inc(ml_ready, 1)
                        n += 1
            pe.wait_ge(conv_silu, 4)
            for g in range(G):
                ps = misc(M_CB + g)
                for s in range(T):
                    mm = nc.tensor.matmul(ps[:, s * S:(s + 1) * S], xbc[:, g, s * P:(s + 1) * P],
                                          xbc[:, G + g, :], start=True, stop=True)
                mm.then_inc(misc_ready, 1)
            pe.wait_ge(conv_silu, 8)
            for m in range(4):
                ps = misc(M_XS + m)
                t, half = m // 2, m % 2
                for j in range(4):
                    mm = nc.tensor.transpose(ps[:, j * P:(j + 1) * P],
                                             xbc[:, 8 + 4 * half + j, t * P:(t + 1) * P], ident[:])
                mm.then_inc(misc_ready, 1)
            decays(1)
            for g in range(G):
                fam = 1 + g
                if g < G - 1:
                    decays(fam + 1)
                rows(OSTEP + g)
                pe.wait_ge(weight_ready, (fam + 1) * NB)
                pe.wait_ge(xdt_ready, 4)
                for t in range(T):
                    if g == 0:
                        pe.wait_ge(ml_read, 16)
                    else:
                        pe.wait_ge(ssm_read, 2 * (g - 1) + t + 1)
                    for j in range(4):
                        parts = [(d, b) for d in range(2) for b in SRC[d, t]]
                        for i, (d, b) in enumerate(parts):
                            col = (4 * g + j) * HP
                            mm = nc.tensor.matmul(bank[6 + t][:, j * HP:(j + 1) * HP], W[fam % 2][b][:, j, :],
                                                  xdt[:, d, BLOCKS[b][1], col:col + HP], start=(i == 0),
                                                  stop=(i == len(parts) - 1))
                    mm.then_inc(ssm_ready, 1)
            for m in range(8):
                if m % 4 == 0:
                    pe.wait_ge(y_ready, 1 + m // 4)
                ps = misc(M_Y + m)
                for c in range(2):
                    for t in range(T):
                        col = (2 * m + c) % 8 * P
                        mm = nc.tensor.transpose(ps[:, (2 * c + t) * P:(2 * c + t + 1) * P],
                                                 (hml if m < 4 else xs)[:, t, col:col + P], ident[:])
                mm.then_inc(misc_ready, 1)
            pe.wait_ge(proj_evac, OSTEP + 3)
            pe.wait_ge(weight_ready, 5 * NB)
            for n in range(10, 13):
                full(n)
                for k in range(6 * (n - 10), min(6 * (n - 10) + 6, 2 * KD)):
                    if k % 2 == 0:
                        pe.wait_ge(misc_evac, M_Y + k // 2 + 1)
                    w = slot[n % RING1].rearrange("p (k c) -> p k c", c=D)
                    for t in range(T):
                        for half in range(2):
                            mm = nc.tensor.matmul(bank[2 * t + half][:, :], yT[:, k, t * P:(t + 1) * P],
                                                  w[:, k - 6 * (n - 10), half * 512:(half + 1) * 512],
                                                  start=(k == 0), stop=(k == 2 * KD - 1))
                mm.then_inc(mix_used, 1)
            pe.wait_ge(h_ready, T)
            for m in range(4):
                ps = misc(M_H + m)
                for c in range(2):
                    for t in range(T):
                        mm = nc.tensor.transpose(ps[:, (2 * c + t) * P:(2 * c + t + 1) * P],
                                                 h[:, t, (2 * m + c) * P:(2 * m + c + 1) * P], ident[:])
                mm.then_inc(misc_ready, 1)
            pe.wait_ge(misc_evac, M_H + 4)
            pe.wait_ge(s_wr, 16)
            for t in range(T):
                for k in range(KD):
                    mm = nc.tensor.matmul(bank[3][:, t * E:(t + 1) * E], hT[:, k, t * P:(t + 1) * P], wr[:, k, :],
                                          start=(k == 0), stop=(k == KD - 1))
            mm.then_inc(logit_ready, 1)
            full(13)
            w = slot[13 % RING1]
            wgu = w[:, 0:KD * 512].rearrange("p (k c) -> p k c", c=512)
            wdn = w[:, KD * 512:].rearrange("p (f c) -> p f c", f=2)
            for t in range(T):
                for k in range(KD):
                    mm = nc.tensor.matmul(bank[t][:, :], hT[:, k, t * P:(t + 1) * P], wgu[:, k, :],
                                          start=(k == 0), stop=(k == KD - 1))
                mm.then_inc(sh_gu, 1)
            for t in range(T):
                pe.wait_ge(sh_hh, t + 1)
                for f in range(2):
                    mm = nc.tensor.transpose(bank[2][:, (2 * f + t) * P:(2 * f + t + 1) * P],
                                             hh[:, t, f * P:(f + 1) * P], ident[:])
            mm.then_inc(sh_tr, 1)
            pe.wait_ge(sh_hhT, 1)
            for f in range(2):
                for t in range(T):
                    for half in range(2):
                        mm = nc.tensor.matmul(bank[4 + 2 * t + half][:, :], hhT[:, f, t * P:(t + 1) * P],
                                              wdn[:, f, half * 512:(half + 1) * 512],
                                              start=(f == 0), stop=False, skip_group_check=True)
            mm.then_inc(sh_used, 1)

            for t in range(T):
                pe.wait_ge(sel_bf, t + 1)
            for t in range(T):
                for i in range(t + 1):
                    nc.tensor.matmul(bank[3][:, 128 + t * E:128 + (t + 1) * E], (before if i == t else onesb)[:],
                                     selb[:, i, :], start=(i == 0), stop=(i == t))
            for i in range(T):
                mm = nc.tensor.matmul(bank[3][:, 256:256 + E], onesb[:], selb[:, i, :],
                                      start=(i == 0), stop=(i == T - 1))
            mm.then_inc(rank_ready, 1)

            def gather(p1, v, half):
                for k in range(4 * half, 4 * half + 4):
                    for t in range(T):
                        for i in range(3):
                            mm = nc.tensor.matmul(bank[1][:, (k % 4) * P:(k % 4 + 1) * P],
                                                  h_part[i][:, t, k * P:(k + 1) * P], onehotb[v][:, t, :],
                                                  start=(t == 0 and i == 0), stop=(t == T - 1 and i == 2))
                mm.then_inc(gather_ready, 1)

            def scatter():
                for i, part in enumerate((y_hi, y_lo)):
                    for t in range(T):
                        for half in range(2):
                            nc.tensor.matmul(bank[4 + 2 * t + half][:, :], onehotT[last][:, t, :],
                                             part[:, half * 512:(half + 1) * 512],
                                             start=False, stop=False, skip_group_check=True)

            pe.wait_ge(h_split, 4)
            pe.wait_ge(onehot_ready, 1)
            gather(0, 0, 0)
            pe.wait_ge(gathered, 1)
            gather(0, 0, 1)
            pe.wait_ge(empty_ready, 1)
            pe.wait_ge(rounds_ready, 1)
            n_rounds = pe.value_load(rounds[0:1, 0:1], min_val=PAIRS // 2, max_val=PASSES * PAIRS // 2)
            with pe.Fori(0, n_rounds) as j:
                for v in range(2):
                    p = j * 2 + v
                    last = 1 - v
                    pe.wait_ge(onehot_ready, p + 2)
                    pe.wait_ge(gathered, p * 2 + 2)
                    pe.wait_ge(hidT_read, p + 1)
                    gather(p + 1, 1 - v, 0)
                    pe.wait_ge(hidden_ready, p + 1)
                    for e in range(2):
                        s = PAIR_SLOTS[v][e]
                        pe.wait_ge(slot_full[s], (j + (loads_in[s] + 1)) * 16)
                    for k in range(KD):
                        for e in range(2):
                            wk = slot[PAIR_SLOTS[v][e]][:, k * 512:(k + 1) * 512]
                            mm = nc.tensor.matmul(bank[0][e * M:(e + 1) * M, :], hc[v][:, k, e * M:(e + 1) * M], wk,
                                                  start=(k == 0), stop=(k == KD - 1))
                        if k == 2:
                            pe.wait_ge(gathered, p * 2 + 3)
                            gather(p + 1, 1 - v, 1)
                        if k == 5:
                            pe.wait_ge(gathered, p * 2 + 4)
                            for t in range(T):
                                nc.tensor.transpose(bank[1][:, t * P:(t + 1) * P],
                                                    onehot[v][:, t, :], ident[:])
                            for t in range(T):
                                tr = nc.tensor.matmul(bank[1][:, 256:258], onehot[v][:, t, :],
                                                      gate[:, t, bass.ds(p * 2, 2)], start=(t == 0), stop=(t == T - 1))
                            tr.then_inc(slotT_ready, 1)
                    mm.then_inc(gu_ready, 1)
                    pe.wait_ge(ylo_ready, p * 2 + 2)
                    scatter()
                    pe.wait_ge(slotT_read, p + 1)
                    pe.wait_ge(hidden_ready, p + 2)
                    for f in range(2):
                        mm = nc.tensor.transpose(bank[1][:, f * P:(f + 1) * P], phh[:, f * P:(f + 1) * P], ident[:])
                    mm.then_inc(hidT_ready, 1)
                    pe.wait_ge(hidT_read, p + 2)
                    for half in range(2):
                        for f in range(2):
                            for e in range(2):
                                c = KD * 512 + f * D + half * 512
                                mm = nc.tensor.matmul(bank[2 + half][e * M:(e + 1) * M, :],
                                                      phhT[:, f, e * M:(e + 1) * M],
                                                      slot[PAIR_SLOTS[v][e]][:, c:c + 512],
                                                      start=(f == 0), stop=(f == 1))
                        mm.then_inc(down_ready, 1)
            pe.wait_ge(ylo_ready, n_rounds * 4 + 2)
            last = 1
            scatter()
            for i in range(4):
                mm = nc.tensor.matmul(bank[4 + i][:, :], zb[:], zb[:, 0:1].to_broadcast([P, 512]),
                                      start=False, stop=True, skip_group_check=True)
            mm.then_inc(moe_ready, 1)

        @block.scalar
        def _(act):
            act.wait_ge(s_const, 176)
            act.wait_ge(gates_z, 1)
            nc.scalar.activation(g_u, g_nz, ACT.Exp).then_inc(gates_u, 1)
            nc.scalar.activation(ea[:], rc[:, 2:3], ACT.Exp).then_inc(gates_u, 1)

            def evac(n, dst, src, scale=1.0, func=ACT.Copy):
                act.wait_ge(proj_ready, n + 1)
                nc.scalar.activation(dst, src, func, scale=scale).then_inc(proj_evac, 1)

            def pair(n):
                return bank[n % 2][:, :].rearrange("p (j t) -> p j t", j=2)

            evac(1, qT[:, 0:2, :], pair(1))
            evac(2, qT[:, 2:4, :], pair(2))
            evac(3, kT[:, 0:2, :], pair(3), scale=DQK ** -0.5)
            evac(4, kT[:, 2:4, :], pair(4), scale=DQK ** -0.5)
            act.wait_ge(em_arg, 1)
            nc.scalar.activation(g_tr[0:64, :], g_m[0:64, :], ACT.Exp).then_inc(em_ready, 1)
            act.wait_ge(pads_ready, 5)
            for n in range(CPAIR + 4, VSTEP):
                c = 2 * (n - CPAIR - 4)
                evac(n, xpad[:, c:c + 2, 2:S + 2], pair(n))

            def conv_act(m):
                act.wait_ge(conv_done, 2 * m + 2)
                nc.scalar.activation(xbc[:, 2 * m:2 * m + 2, :], xbc[:, 2 * m:2 * m + 2, :],
                                     ACT.Silu).then_inc(conv_silu, 1)

            def decay_exps(fam):
                for n in range(fam * NB, (fam + 1) * NB):
                    act.wait_ge(decay_ready, n + 1)
                    ps = bank[2 + n % 2]
                    nc.scalar.activation(ps[:, :], ps[:, :], ACT.Exp).then_inc(decay_exp, 1)

            for m in range(4):
                conv_act(m)
            for n in range(VSTEP, ZSTEP):
                blk, t = (n - VSTEP) // 2, (n - VSTEP) % 2
                evac(n, vext[:, t, 2 * blk:2 * blk + 2, 0:DV], pair(n))
            decay_exps(0)
            for n in range(ZSTEP, OSTEP):
                blk, t = (n - ZSTEP) // 2, (n - ZSTEP) % 2
                evac(n, zs[:, t, blk * 512:(blk + 1) * 512], bank[n % 2][:, :], func=ACT.Silu)
            for m in range(4, 8):
                conv_act(m)
            decay_exps(1)
            act.wait_ge(ml_ready, 16)
            for g in range(G):
                if g < G - 1:
                    decay_exps(g + 2)
                n = OSTEP + g
                blk, t = g // 2, g % 2
                evac(n, osig[:, t, blk * 512:(blk + 1) * 512], bank[n % 2][:, :])
            act.wait_ge(proj_evac, OSTEP + 3)
            nc.scalar.activation(at(O_V, T * D), at(O_V, T * D), ACT.Sigmoid).then_inc(o_sig, 1)
            for t in range(T):
                act.wait_ge(y_gated, t + 1)
                for g in range(G):
                    sq = nc.scalar.activation(bank[7][:, 0:256], xs[:, t, g * 256:(g + 1) * 256], ACT.Square,
                                              accum_out=ssq[:, t, g:g + 1])
                    sq.then_inc(sq_done, 1)
                    act.wait_ge(sq_done, t * G + g + 1)
            for i in range(2):
                w = 16 if i == 0 else T
                act.wait_ge(var_ready, i + 1)
                nc.scalar.activation(vv[:, 1, 0:w], vv[:, 0, 0:w], ACT.Sqrt).then_inc(sqrt_done, 1)
            act.wait_ge(h_ready, T)
            nc.scalar.activation(h_part[0][:], h[:], ACT.Copy).then_inc(h_split, 1)
            act.wait_ge(h_split, 2)
            nc.scalar.activation(h_part[1][:], h_rest[:], ACT.Copy).then_inc(h_split, 1)
            act.wait_ge(logit_ready, 1)
            nc.scalar.activation(score[:, :, :], bank[3][:, 0:T * E].rearrange("p (t e) -> p t e", t=T),
                                 ACT.Sigmoid).then_inc(score_ready, 1)

            for t in range(T):
                act.wait_ge(sh_gu, t + 1)
                nc.scalar.activation(sg[:, t, :], bank[t][:, 0:FE], ACT.Silu).then_inc(sh_silu, 1)
            nc.scalar.activation(y_hi[:], zb[:, 0:1].to_broadcast([P, D]), ACT.Copy).then_inc(yhi_ready, 1)

            def gather_copy(n, v, half):
                act.wait_ge(gather_ready, n)
                nc.scalar.activation(hc[v][:, 4 * half:4 * half + 4, :],
                                     bank[1][:, :].rearrange("p (k c) -> p k c", k=4), ACT.Copy).then_inc(gathered, 1)

            gather_copy(1, 0, 0)
            gather_copy(2, 0, 1)
            act.wait_ge(rounds_ready, 1)
            n_rounds = act.value_load(rounds[0:1, 0:1], min_val=PAIRS // 2, max_val=PASSES * PAIRS // 2)
            with act.Fori(0, n_rounds) as j:
                for v in range(2):
                    p = j * 2 + v
                    gather_copy(p * 2 + 3, 1 - v, 0)
                    gather_copy(p * 2 + 4, 1 - v, 1)
                    act.wait_ge(gu_ready, p + 1)
                    act.wait_ge(hidden_ready, p + 1)
                    nc.scalar.activation(psg, bank[0][:, 0:FE], ACT.Silu).then_inc(silu_done, 1)
                    for half in range(2):
                        act.wait_ge(down_ready, p * 2 + (half + 1))
                        nc.scalar.activation(y_hi[:, half * 512:(half + 1) * 512], bank[2 + half][:, :],
                                             ACT.Copy).then_inc(yhi_ready, 1)
            act.wait_ge(var_ready, 3)
            nc.scalar.activation(vv[:, 1, 0:T], vv[:, 0, 0:T], ACT.Sqrt).then_inc(sqrt_done, 1)

        @block.vector
        def _(dve):
            V = nc.vector
            chain = [0]

            def link(ins):
                ins.then_inc(s_dve, 1)
                chain[0] += 1
                dve.wait_ge(s_dve, chain[0])

            dve.wait_ge(s_const, 176)
            dve.wait_ge(proj_ready, 1)
            link(V.tensor_scalar(g_z, bank[0][0:R, 0:S], rc[:, 0:1], rc[:, 1:2], ALU.add, ALU.mult))
            V.tensor_scalar(g_it, bank[0][0:R, S:2 * S], rc[:, 7:8], None, ALU.add).then_inc(gate_read, 1)
            V.scalar_tensor_tensor(out=g_nz, in0=g_z, scalar=-1.0, in1=g_z, op0=ALU.mult,
                                   op1=ALU.min).then_inc(gates_z, 1)
            link(V.memset(g_zero, 0.0))
            dve.wait_ge(gates_u, 2)
            link(V.tensor_scalar(g_w, g_u, 2.0, None, ALU.add))
            link(V.reciprocal(g_r, g_w))
            link(V.tensor_tensor(g_s, g_u, g_r, ALU.mult))
            link(V.tensor_tensor(g_s2, g_s, g_s, ALU.mult))
            link(V.tensor_scalar(g_p, g_s2, 1.0 / 17.0, None, ALU.mult))
            for k in range(15, 2, -2):
                link(V.scalar_tensor_tensor(out=g_p, in0=g_p, scalar=1.0 / k, in1=g_s2, op0=ALU.add, op1=ALU.mult))
            link(V.scalar_tensor_tensor(out=g_p, in0=g_p, scalar=1.0, in1=g_s, op0=ALU.add, op1=ALU.mult))
            link(V.tensor_scalar(g_w, g_z, 0.0, None, ALU.max))
            link(V.scalar_tensor_tensor(out=g_sp, in0=g_p, scalar=2.0, in1=g_w, op0=ALU.mult, op1=ALU.add))
            link(V.tensor_scalar(mcol[:], ea[:], -1.0, None, ALU.mult))
            link(V.tensor_scalar(g_dec, g_sp, mcol[:], None, ALU.mult))
            link(V.tensor_tensor_scan(g_cum[:, 0:P], g_dec[:, 0:P], g_zero[:, 0:P], 0.0, ALU.add, ALU.add))
            link(V.tensor_tensor(inic[:], g_cum[:, P - 1:P], rc[:, 5:6], ALU.mult))
            link(V.tensor_tensor_scan(g_cum[:, P:S], g_dec[:, P:S], g_zero[:, P:S], inic[:], ALU.add, ALU.add))
            link(V.tensor_scalar(g_x, g_cum, rc[:, 3:4], None, ALU.mult))
            link(V.scalar_tensor_tensor(out=g_x, in0=g_dec, scalar=rc[:, 4:5], in1=g_x, op0=ALU.mult, op1=ALU.add))
            link(V.tensor_tensor(g0m[:], g_cum[:, P - 1:P], rc[:, 6:7], ALU.mult))
            link(V.tensor_tensor(col_d, g_it, g_x, ALU.subtract))
            link(V.tensor_scalar(col_o, col_d, g0m[:], None, ALU.add))
            link(V.memset(g_m[0:64, :], 0.0))
            link(V.tensor_tensor_scan(g_m[0:H, :], col_d[0:H, :], col_d[0:H, :], NEG, ALU.max, ALU.max))
            link(V.tensor_tensor_scan(g_m[32:32 + H, ::-1], col_d[32:32 + H, ::-1], col_d[32:32 + H, ::-1],
                                      NEG, ALU.max, ALU.max))
            link(V.tensor_scalar(row_t[0:64, :], g_m[0:64, :], -1.0, None, ALU.mult))
            link(V.tensor_copy(row_t[64:R, :], g_x[64:R, :]))
            V.tensor_tensor(g_m[0:64, :], row_t[0:64, :], g_x[0:64, :], ALU.subtract).then_inc(em_arg, 1)
            V.tensor_copy(g_tr[64:R, :], g_sp[64:R, :]).then_inc(rows_ready, 1)

            def misc_copy(m, dst, src):
                dve.wait_ge(misc_ready, m + 1)
                V.tensor_copy(dst, src).then_inc(misc_evac, 1)

            def mbank(m, n):
                return bank[4 + m % 2][:, :].rearrange("p (j t) -> p j t", j=n)

            def conv(c):
                link(V.tensor_scalar(xbc[:, c, :], xpad[:, c, 0:S], convw[:, c, 0:1], convb[:, c:c + 1],
                                     ALU.mult, ALU.add))
                for k in range(1, TAPS):
                    ins = V.scalar_tensor_tensor(out=xbc[:, c, :], in0=xpad[:, c, k:k + S],
                                                 scalar=convw[:, c, k:k + 1], in1=xbc[:, c, :],
                                                 op0=ALU.mult, op1=ALU.add)
                    if k < TAPS - 1:
                        link(ins)
                ins.then_inc(conv_done, 1)

            def weights(fam):
                if fam == 2:
                    dve.wait_ge(ml_ready, 16)
                elif fam > 2:
                    dve.wait_ge(ssm_ready, 2 * (fam - 2))
                for b, (d, s, t, _) in enumerate(BLOCKS):
                    n = fam * NB + b
                    dve.wait_ge(decay_exp, n + 1)
                    e = bank[2 + n % 2][:, :].rearrange("p (j t) -> p j t", j=4)
                    if fam == 0:
                        sc = st[:, :, s, t * P:(t + 1) * P]
                    else:
                        sc = cb[:, fam - 1, s:s + 1, t * P:(t + 1) * P].to_broadcast([P, 4, P])
                    V.tensor_tensor(W[fam % 2][b], e, sc, ALU.mult).then_inc(weight_ready, 1)

            misc_copy(M_COL, colT[:], mbank(M_COL, 4)[:, 0:T, 0:R])
            for hd in range(H):
                misc_copy(M_ST + hd, st[:, hd, :, :], mbank(M_ST + hd, 2))
            for c in range(8):
                dve.wait_ge(proj_evac, CPAIR + 4 + c // 2)
                conv(c)
            weights(0)
            for c in range(8, CT):
                dve.wait_ge(proj_evac, CPAIR + 4 + c // 2)
                conv(c)
            n = 0
            for t in range(T):
                for hd in range(H):
                    for d in range(2):
                        ps = bank[6 + n % 2]
                        dst = hml[:, t, hd * DV:(hd + 1) * DV]
                        c = ROW0[d] + hd
                        dve.wait_ge(ml_ready, n + 1)
                        link(V.tensor_scalar(dcol[:, 0:1], ps[:, DV:DV + 1], colT[:, t, c:c + 1], None, ALU.max))
                        link(V.scalar_tensor_tensor(out=dcol[:, 0:1], in0=ps[:, DV:DV + 1], scalar=-1.0,
                                                    in1=dcol[:, 0:1], op0=ALU.mult, op1=ALU.max))
                        link(V.reciprocal(dcol[:, 1:2], dcol[:, 0:1]))
                        if d == 0:
                            ins = V.tensor_scalar(dst, ps[:, 0:DV], dcol[:, 1:2], None, ALU.mult)
                        else:
                            ins = V.scalar_tensor_tensor(out=dst, in0=ps[:, 0:DV], scalar=dcol[:, 1:2], in1=dst,
                                                         op0=ALU.mult, op1=ALU.add)
                        ins.then_inc(ml_read, 1)
                        n += 1
                        dve.wait_ge(ml_read, n)
            for g in range(G):
                misc_copy(M_CB + g, cb[:, g, :, :], mbank(M_CB + g, 2))
            for m in range(4):
                misc_copy(M_XS + m, xs[:, m // 2, (m % 2) * 512:(m % 2 + 1) * 512], bank[4 + (M_XS + m) % 2][:, :])
            dve.wait_ge(misc_evac, M_XS + 4)
            for d in range(2):
                for t in range(T):
                    q = ROW0[2 + d]
                    V.tensor_tensor(xdt[:, d, t, :].rearrange("p (h c) -> p h c", h=SH),
                                    xs[:, t, :].rearrange("p (h c) -> p h c", h=SH),
                                    colT[:, t, q:q + SH].unsqueeze(2).to_broadcast([P, SH, HP]),
                                    ALU.mult).then_inc(xdt_ready, 1)
            dve.wait_ge(xdt_ready, 4)
            for t in range(T):
                v = xs[:, t, :].rearrange("p (h c) -> p h c", h=SH)
                link(V.tensor_tensor(v, v, dsk[:].unsqueeze(2).to_broadcast([P, SH, HP]), ALU.mult))
            weights(1)
            for g in range(G):
                if g < G - 1:
                    weights(g + 2)
                for t in range(T):
                    dve.wait_ge(ssm_ready, 2 * g + t + 1)
                    v = xs[:, t, g * 256:(g + 1) * 256]
                    V.tensor_tensor(v, bank[6 + t][:, 0:256], v, ALU.add).then_inc(ssm_read, 1)
            dve.wait_ge(ssm_read, 2 * G)
            dve.wait_ge(proj_evac, OSTEP - 1)
            for t in range(T):
                V.tensor_tensor(xs[:, t, :], xs[:, t, :], zs[:, t, :], ALU.mult).then_inc(y_gated, 1)

            def rsqrt(w, count):
                link(V.tensor_copy(vv[:, 2, 0:w], vv[:, 0, 0:w]))
                dve.wait_ge(sqrt_done, count)
                link(V.reciprocal(vv[:, 3, 0:w], vv[:, 1, 0:w]))
                link(V.tensor_tensor(vv[:, 4, 0:w], vv[:, 3, 0:w], vv[:, 3, 0:w], ALU.mult))
                link(V.tensor_tensor(vv[:, 4, 0:w], vv[:, 4, 0:w], vv[:, 2, 0:w], ALU.mult))
                link(V.tensor_scalar(vv[:, 4, 0:w], vv[:, 4, 0:w], -0.5, 1.5, ALU.mult, ALU.add))
                link(V.tensor_tensor(vv[:, 3, 0:w], vv[:, 3, 0:w], vv[:, 4, 0:w], ALU.mult))

            for i in range(8):
                ins = V.bn_stats(stat[:, i, :], hml[:, i // H, (i % H) * DV:(i % H + 1) * DV])
            link(ins)
            for i in range(8):
                ins = V.bn_aggr(mv[:, i, :], stat[:, i, :])
            link(ins)
            link(V.tensor_scalar(vv[:, 0, 0:8], mv[:, :, 1], EPS, None, ALU.add))
            dve.wait_ge(sq_done, T * G)
            V.tensor_scalar(vv[:, 0, 8:16], ssq[:].rearrange("p t g -> p (t g)"), 1.0 / 256, EPS, ALU.mult,
                            ALU.add).then_inc(var_ready, 1)
            dve.wait_ge(var_ready, 1)
            rsqrt(16, 1)
            for i in range(8):
                v = hml[:, i // H, (i % H) * DV:(i % H + 1) * DV]
                ins = V.tensor_scalar(v, v, mv[:, i, 0:1], vv[:, 3, i:i + 1], ALU.subtract, ALU.mult)
            link(ins)
            dve.wait_ge(o_sig, 1)
            for t in range(T):
                link(V.tensor_tensor(hml[:, t, :], hml[:, t, :], nrm[:, 0, :], ALU.mult))
                ins = V.tensor_tensor(hml[:, t, :], hml[:, t, :], osig[:, t, :], ALU.mult)
                if t == 0:
                    link(ins)
            ins.then_inc(y_ready, 1)
            for i in range(8):
                v = xs[:, i // G, (i % G) * 256:(i % G + 1) * 256]
                n = nrm[:, 1, (i % G) * 256:(i % G + 1) * 256]
                ins = V.scalar_tensor_tensor(out=v, in0=v, scalar=vv[:, 3, 8 + i:9 + i], in1=n,
                                             op0=ALU.mult, op1=ALU.mult)
            ins.then_inc(y_ready, 1)
            for m in range(8):
                misc_copy(M_Y + m, yT[:, 2 * m:2 * m + 2, :], mbank(M_Y + m, 2))

            def layer_norm(src, dst, which, count, signal, first_bank):
                for t in range(T):
                    for half in range(2):
                        c = slice(half * 512, (half + 1) * 512)
                        link(V.scalar_tensor_tensor(out=dst[:, t, c], in0=src[:, t, c], scalar=ALPHA,
                                                    in1=bank[first_bank + 2 * t + half][:, :],
                                                    op0=ALU.mult, op1=ALU.add))
                        link(V.bn_stats(stat[:, 2 * t + half, :], dst[:, t, c]))
                    link(V.bn_aggr(mv[:, t, :], stat[:, 2 * t:2 * t + 2, :].rearrange("p a b -> p (a b)")))
                V.tensor_scalar(vv[:, 0, 0:T], mv[:, 0:T, 1], EPS, None, ALU.add).then_inc(var_ready, 1)
                dve.wait_ge(var_ready, count)
                rsqrt(T, count)
                for t in range(T):
                    v = dst[:, t, :]
                    link(V.tensor_scalar(v, v, mv[:, t, 0:1], vv[:, 3, t:t + 1], ALU.subtract, ALU.mult))
                    link(V.tensor_tensor(v, v, ln[:, 2 * which, :], ALU.mult))
                    V.tensor_tensor(v, v, ln[:, 2 * which + 1, :], ALU.add).then_inc(signal, 1)
                dve.wait_ge(signal, T)

            dve.wait_ge(mix_used, 3)
            dve.wait_ge(s_xin, 16)
            dve.wait_ge(s_late, 16)
            layer_norm(xin, h, 0, 2, h_ready, 0)
            for m in range(4):
                misc_copy(M_H + m, hT[:, 2 * m:2 * m + 2, :], mbank(M_H + m, 2))

            def top_k(dst, vals, thr, k, w):
                link(V.tensor_scalar(sel[:, 0, 0:w], vals, thr, None, ALU.is_gt, ALU.add, accum_out=need[:, 0:1]))
                link(V.tensor_scalar(need[:, 1:2], need[:, 0:1], -1.0, float(k), ALU.mult, ALU.add))
                link(V.tensor_scalar(sel[:, 1, 0:w], vals, thr, None, ALU.is_equal))
                link(V.tensor_tensor_scan(sel[:, 2, 0:w], sel[:, 1, 0:w], zero64[:, 0:w], 0.0, ALU.add, ALU.add))
                link(V.scalar_tensor_tensor(out=sel[:, 1, 0:w], in0=sel[:, 2, 0:w], scalar=need[:, 1:2],
                                            in1=sel[:, 1, 0:w], op0=ALU.is_le, op1=ALU.mult))
                link(V.tensor_tensor(dst, sel[:, 0, 0:w], sel[:, 1, 0:w], ALU.add))

            dve.wait_ge(h_split, 1)
            V.tensor_tensor(h_rest[:], h[:], h_part[0][:], ALU.subtract).then_inc(h_split, 1)
            dve.wait_ge(h_split, 3)
            V.tensor_tensor(h_part[2][:], h_rest[:], h_part[1][:], ALU.subtract).then_inc(h_split, 1)
            for t in range(T):
                dve.wait_ge(sh_silu, t + 1)
                V.tensor_tensor(hh[:, t, :], sg[:, t, :], bank[t][:, FE:2 * FE], ALU.mult).then_inc(sh_hh, 1)
            link(V.memset(zero64, 0.0))
            dve.wait_ge(score_ready, 1)
            for t in range(T):
                link(V.tensor_tensor(choice, score[:, t, :], rbias[:], ALU.add))
                for g in range(EG):
                    ins = V.max(top8[:, g, :], choice[:, g * 8:(g + 1) * 8])
                link(ins)
                link(V.tensor_tensor(gsc[:, 0, :], top8[:, :, 0], top8[:, :, 1], ALU.add))
                link(V.max(gt8[:], gsc[:, 0, :]))
                top_k(gsc[:, 1, :], gsc[:, 0, :], gt8[:, TOPG - 1:TOPG], TOPG, EG)
                gm = gsc[:, 1, :].unsqueeze(2).to_broadcast([P, EG, 8])
                c3 = cand.rearrange("p (g e) -> p g e", g=EG)
                link(V.tensor_tensor(c3, choice.rearrange("p (g e) -> p g e", g=EG), gm, ALU.mult))
                link(V.tensor_scalar(gsc[:, 0, :], gsc[:, 1, :], BIG, -BIG, ALU.mult, ALU.add))
                link(V.tensor_tensor(c3, c3, gsc[:, 0, :].unsqueeze(2).to_broadcast([P, EG, 8]), ALU.add))
                link(V.max(gt8[:], cand))
                top_k(sel[:, 3, :], cand, gt8[:, TOPK - 1:TOPK], TOPK, E)
                V.tensor_copy(selb[:, t, :], sel[:, 3, :]).then_inc(sel_bf, 1)
                link(V.tensor_tensor(cand, sel[:, 3, :], score[:, t, :], ALU.mult))
                link(V.tensor_reduce(need[:, 0:1], cand, AX_X, ALU.add))
                link(V.reciprocal(need[:, 1:2], need[:, 0:1]))
                for b in range(PASSES):
                    ins = V.tensor_scalar(gate[:, t, b * E:(b + 1) * E], cand, need[:, 1:2], ROUTED_SCALE, ALU.mult,
                                          ALU.mult)
                link(ins)
                if t == 0:
                    dve.wait_ge(sh_tr, 1)
                    V.tensor_copy(hhT[:], bank[2][:, :].rearrange("p (f t) -> p f t", f=2)).then_inc(sh_hhT, 1)
            dve.wait_ge(rank_ready, 1)
            link(V.tensor_reduce(rounds_f[:, 0:1], bank[3][:, 256:256 + E], AX_X, ALU.max))
            link(V.memset(rounds_f[:, 1:2], PAIRS / 2))
            for b in range(1, PASSES):
                link(V.tensor_scalar(need[:, 0:1], rounds_f[:, 0:1], float(b * M), PAIRS / 2, ALU.is_gt, ALU.mult))
                link(V.tensor_tensor(rounds_f[:, 1:2], rounds_f[:, 1:2], need[:, 0:1], ALU.add))
            V.tensor_copy(rounds[:], rounds_f[0:1, 1:2]).then_inc(rounds_ready, 1)
            link(V.memset(rk[:, :, PASSES * E:], -1.0))
            for t in range(T):
                link(V.tensor_scalar(rk[:, t, 0:E], bank[3][:, 128 + t * E:128 + (t + 1) * E], 1.0, None, ALU.add))
                link(V.tensor_tensor(rk[:, t, 0:E], rk[:, t, 0:E], selb[:, t, :], ALU.mult))
                link(V.tensor_scalar(rk[:, t, 0:E], rk[:, t, 0:E], -1.0, None, ALU.add))
                for b in range(1, PASSES):
                    ins = V.tensor_scalar(rk[:, t, b * E:(b + 1) * E], rk[:, t, 0:E], -float(b * M), None, ALU.add)
                link(ins)

            def one_hot(p, v):
                dst = onehot[v][:, :, :].rearrange("p t (e m) -> p t e m", e=2)
                num = rk[:, :, 2 * p:2 * p + 2] if isinstance(p, int) else rk[:, :, bass.ds(p * 2, 2)]
                V.tensor_tensor(dst, iota.unsqueeze(1).unsqueeze(1).to_broadcast([P, T, 2, M]),
                                num.unsqueeze(3).to_broadcast([P, T, 2, M]), ALU.is_equal).then_inc(onehot_made, 1)
                dve.wait_ge(onehot_made, p + 1)
                V.tensor_copy(onehotb[v][:], onehot[v]).then_inc(onehot_ready, 1)

            dve.wait_ge(iota_ready, 1)
            one_hot(0, 0)
            one_hot(1, 1)
            dve.wait_ge(yhi_ready, 1)
            V.memset(onehotT[1][:].bitcast(F32), 0.0).then_inc(empty_ready, 1)
            V.tensor_copy(y_lo[:], y_hi[:].bitcast(F32)).then_inc(ylo_ready, 2)
            V.memset(rounds_f[:, 0:1], 0.0).then_inc(hidT_read, 1)
            V.memset(rounds_f[:, 1:2], 0.0).then_inc(hidden_ready, 1)
            dve.wait_ge(rounds_ready, 1)
            n_rounds = dve.value_load(rounds[0:1, 0:1], min_val=PAIRS // 2, max_val=PASSES * PAIRS // 2)
            with dve.Fori(0, n_rounds) as j:
                for v in range(2):
                    p = j * 2 + v
                    dve.wait_ge(slotT_ready, p + 1)
                    V.tensor_copy(gcol[0:M, :], bank[1][0:M, 256:257])
                    V.tensor_copy(gcol[M:P, :], bank[1][M:P, 257:258])
                    V.tensor_copy(onehotT[v][:], bank[1][:, 0:S].rearrange("p (t s) -> p t s", t=T)
                                  ).then_inc(slotT_read, 1)
                    one_hot(p + 2, v)
                    dve.wait_ge(silu_done, p + 1)
                    dve.wait_ge(slotT_read, p + 1)
                    V.scalar_tensor_tensor(out=phh, in0=psg, scalar=gcol, in1=bank[0][:, FE:2 * FE],
                                           op0=ALU.mult, op1=ALU.mult).then_inc(hidden_ready, 1)
                    dve.wait_ge(hidT_ready, p + 1)
                    V.tensor_copy(phhT, bank[1][:, 0:2 * P].rearrange("p (f s) -> p f s", f=2)).then_inc(hidT_read, 1)
                    for half in range(2):
                        dve.wait_ge(yhi_ready, p * 2 + (half + 2))
                        c = slice(half * 512, (half + 1) * 512)
                        V.tensor_tensor(y_lo[:, c], bank[2 + half][:, :], y_hi[:, c].bitcast(F32),
                                        ALU.subtract).then_inc(ylo_ready, 1)
            dve.wait_ge(moe_ready, 1)
            layer_norm(h, ytmp, 1, 3, out_ready, 4)


NAMES = ["wgi", "xT", "wc", "wn", "wo", "ws", "we", "before", "rc", "oneh", "ident", "negm", "convw", "convb", "dsk", "rbias",
         "nrm", "ln", "x", "wr"]


def layout(**v):
    import numpy as np

    f = np.float32
    v = {k: np.asarray(x) for k, x in v.items()}
    x = v["x"][0]
    w = v["w_in"][0]
    q0, k0, v0, o0, i0, f0, z0, c0, d0 = 0, 512, 1024, 2048, 3072, 3080, 3088, 4112, 6160
    rows = lambda m: m.reshape(-1, P, m.shape[1]).transpose(1, 0, 2)
    out = {}
    out["x"] = rows(x).reshape(P, T * D)
    out["xT"] = rows(x.T)
    wgi = np.zeros((D, 2, R), f)
    for d in range(2):
        wgi[:, 0, ROW0[d]:ROW0[d] + H] = w[:, f0 + d * H:f0 + (d + 1) * H]
        wgi[:, 1, ROW0[d]:ROW0[d] + H] = w[:, i0 + d * H:i0 + (d + 1) * H]
        wgi[:, 0, ROW0[2 + d]:ROW0[2 + d] + SH] = w[:, d0 + d * SH:d0 + (d + 1) * SH]
    out["wgi"] = wgi.reshape(KD, P, 2, R).transpose(1, 0, 2, 3)
    rc = np.zeros((R, 8), f)
    rc[0:64, 1] = -1
    rc[64:, 1] = 1
    rc[:, 2] = NEG
    rc[:, 3] = 1
    rc[0:64, 5] = 1
    rc[64:, 6] = 1
    for d in range(2):
        m, s = slice(ROW0[d], ROW0[d] + H), slice(ROW0[2 + d], ROW0[2 + d] + SH)
        rc[m, 0] = v["ml_f_bias"][0, d * H:(d + 1) * H]
        rc[m, 2] = 0
        rc[m, 7] = v["ml_i_bias"][0, d * H:(d + 1) * H]
        rc[s, 0] = v["dt_bias"][0, d * SH:(d + 1) * SH]
        rc[s, 2] = v["a_log"][0, d * SH:(d + 1) * SH]
        if d == 1:
            rc[m, 3] = rc[s, 3] = -1
            rc[m, 4] = rc[s, 4] = 1
    out["rc"] = rc
    xbc_order = np.concatenate([np.arange(D, CH), np.arange(D)])
    chans = np.concatenate([np.arange(q0, v0), c0 + xbc_order])
    wc = w[:, chans].reshape(KD, P, 4, 6, P)
    out["wc"] = wc.transpose(2, 1, 3, 0, 4).reshape(4, P, SLOT)
    wn = np.concatenate([w[:, v0:o0], w[:, z0:c0], w[:, o0:i0]], 1).reshape(KD, P, 6, 512)
    out["wn"] = wn.transpose(2, 1, 0, 3).reshape(6, P, KD * 512)
    out["wo"] = rows(v["w_out"][0]).reshape(P, 2 * KD * D)

    def expert(gate, up, down):
        n = gate.shape[0]
        gu = np.concatenate([gate.reshape(n, KD, P, 1, FE), up.reshape(n, KD, P, 1, FE)], 3)
        dn = down.reshape(n, 2, P, D).transpose(0, 2, 1, 3)
        return np.concatenate([gu.transpose(0, 2, 1, 3, 4).reshape(n, P, KD * 512), dn.reshape(n, P, 2 * D)], 2)

    out["ws"] = expert(v["w_sh_gate"], v["w_sh_up"], v["w_sh_down"])[0]
    out["we"] = expert(v["w_exp_gate"][0], v["w_exp_up"][0], v["w_exp_down"][0])
    oneh = np.zeros((R, SH, P), f)
    for q in ROW0:
        for r in range(min(SH, R - q)):
            oneh[q + r, r, :] = 1
    out["oneh"] = oneh.reshape(R, SH * P)
    out["ident"] = np.eye(P, dtype=f)
    s, t = np.arange(P)[:, None], np.arange(P)[None, :]
    out["negm"] = np.stack([np.where(s <= t, 0, NEG), np.where(s >= t, 0, NEG)], 1).astype(f)
    out["before"] = (s < t).astype(f)
    out["convw"] = v["conv_w"][0][:, xbc_order].reshape(TAPS, CT, P).transpose(2, 1, 0).reshape(P, CT * TAPS)
    out["convb"] = v["conv_b"][0][xbc_order].reshape(CT, P).T
    out["dsk"] = v["d_skip"]
    out["rbias"] = v["router_bias"]
    out["nrm"] = np.concatenate([v["ml_norm_w"], v["ssm_norm_w"]], 1)
    out["ln"] = np.concatenate([v["ln1_g"], v["ln1_b"], v["ln2_g"], v["ln2_b"]], 1)
    out["wr"] = rows(v["w_router"][0])
    return {n: np.ascontiguousarray(out[n]) for n in NAMES}


def kernel(**inputs):
    import concourse.bacc as _bacc
    from concourse import mybir as _mybir
    from concourse.bass_utils import run_bass_kernel_spmd as _run

    nc = _bacc.Bacc("TRN2", target_bir_lowering=False, num_devices=1)
    arrays, args = {}, {}
    for name, arr in layout(**inputs).items():
        arrays[f"in_{name}_dram"] = arr
        args[name] = nc.dram_tensor(f"in_{name}_dram", arr.shape, _mybir.dt.from_np(arr.dtype),
                                    kind="ExternalInput").ap()
    out = nc.dram_tensor("out_0_dram", (1, S, D), _mybir.dt.float32, kind="ExternalOutput").ap()
    build(nc, args, out)
    r = _run(nc, [arrays], core_ids=[0])
    return r.results[0]["out_0_dram"]
```

```python
from contextlib import ExitStack

import concourse.bass as bass
from concourse import mybir

F32 = mybir.dt.float32
F32R = mybir.dt.float32r
BF16 = mybir.dt.bfloat16
I32 = mybir.dt.int32
ALU = mybir.AluOpType
ACT = mybir.ActivationFunctionType
AX_X = mybir.AxisListType.X

P = 128
D = 1024
S = 256
T = S // P
KD = D // P
H = 4
DV = D // H
DQK = DV // 2
SH = 16
G = 4
HP = 64
NST = 128
CH = D + 2 * G * NST
CT = CH // P
TAPS = 5
E = 64
EG = 8
TOPG = 4
TOPK = 8
FE = D // 4
ROUTED_SCALE = 2.5
EPS = 1e-5
ALPHA = 2 ** 0.25
R = P
RD = 64
PARTS = 3
ML0 = PARTS * SH
FAMS = 5
RC = 10
NEG = -1.0e30
BIG = 1.0e30

KIB = 256
SLOT = 24 * KIB
O_RING = 0
O_XT = 72 * KIB
O_XPAD = 80 * KIB
O_XBC = O_XPAD + CT * (S + 4)
O_V = O_XBC + CT * S
O_QK = O_V + T * H * (DV + 1)
O_ST = O_QK + 8 * KIB
O_W = O_ST + 8 * KIB
O_OH = O_W + 24 * KIB
O_CW = O_OH + FAMS * 4 * P // 2
O_PC = O_CW + 128
O_Z = O_OH + 8 * KIB
O_XS = O_Z + 8 * KIB
O_HML = O_XS + 8 * KIB
O_NRM = O_HML + 8 * KIB
O_ROWS = O_NRM + 8 * KIB
O_END = O_ROWS + 3 * KIB

BLOCKS = [(0, 0, 0, True), (0, 0, 1, False), (0, 1, 1, True),
          (1, 0, 0, True), (1, 1, 0, False), (1, 1, 1, True)]
NB = len(BLOCKS)
UNIT = 8 * KIB
CUNITS = 12
RUNITS = 12
OUNITS = 8
UNITS = CUNITS + RUNITS + OUNITS
RING_U = 4
SHARED_SLOT = 0
PAIR_SLOTS = ((3, 2), (0, 1))
PAIRS = E // 2
SPARE = 4
M = P // 2
FIRST_ROUNDS = 8
PASSES = S // M
RKW = PASSES * E + 4


def build(nc, a, out):
    ctx = ExitStack()
    with ctx:
        def sem(name):
            return ctx.enter_context(nc.semaphore(name))

        def small(name, shape, dt=F32):
            return ctx.enter_context(nc.sbuf_tensor(name, shape, dt))

        arena = ctx.enter_context(nc.sbuf_tensor("arena", [P, O_END], F32))
        arena_at = nc.sbuf_base - 4 * O_END

        def rounded(name, off, *dims):
            assert arena_at % 32 == 0
            return nc.alloc_sbuf_tensor_at(name, [P, *dims], F32R, offset=arena_at + 4 * off)

        def at(off, *dims, rows=P):
            n = 1
            for d in dims:
                n *= d
            v = arena[0:rows, off:off + n]
            if len(dims) == 2:
                v = v.rearrange("p (a b) -> p a b", a=dims[0])
            elif len(dims) == 3:
                v = v.rearrange("p (a b c) -> p a b c", a=dims[0], b=dims[1])
            return v

        bank = [ctx.enter_context(nc.psum_tensor(f"bank{i}", [P, 512], F32)) for i in range(8)]

        slot = [at(O_RING + i * SLOT, SLOT) for i in range(3)] + [at(O_W, SLOT)]
        xT = at(O_XT, KD, S)
        unit = [at(O_RING + 2 * i * UNIT, UNIT) for i in range(RING_U)]
        unit_part = [[rounded(f"unit{i}_{part}", O_RING + (2 * i + (part == "hi")) * UNIT, UNIT)
                      for part in ("hi", "lo")] for i in range(RING_U)]
        x_part = [rounded("x_hi", O_RING + 2 * RING_U * UNIT, KD, S), rounded("x_lo", O_XT, KD, S)]
        hT = at(O_XT, KD, S)
        xpad = at(O_XPAD, CT, S + 4)
        xdt = at(O_XPAD, 2, T, D)
        ln = at(O_XPAD, 4, D)
        xbc = at(O_XBC, CT, S)
        y_part = [rounded("yT_hi", O_W, CT, S), rounded("yT_lo", O_XBC, CT, S)]
        vext = at(O_V, T, H, DV + 1)
        osig = at(O_V, T, D)
        qT = at(O_QK, H, S)
        kT = at(O_QK + H * S, H, S)
        cb = at(O_QK, G, T, S)
        st = at(O_ST, H, T, S)
        xin = at(O_ST, T, D)
        W = [[at(O_W + (f * NB + b) * 512, 4, P) for b in range(NB)] for f in range(2)]
        oneh = nc.alloc_sbuf_tensor_at("oneh", [P, FAMS * 4, P], BF16, offset=arena_at + 4 * O_OH)
        expo = nc.alloc_sbuf_tensor_at("expo", [P, 3, S], BF16, offset=arena_at + 4 * O_PC)
        exact = at(O_ROWS, 3, S)
        zs = at(O_Z, T, D)
        xs = at(O_XS, T, D)
        hml = at(O_HML, T, D)
        h = hml
        nrm = at(O_NRM, 2, D)
        col_d = at(O_ROWS, S, rows=R)
        col_o = at(O_ROWS + S, S, rows=R)
        row_t = at(O_ROWS + 2 * S, S, rows=R)
        tmp = [at(O_W + i * S, S, rows=R) for i in range(16)]
        g_z, g_nz, g_u, g_w, g_r, g_s, g_s2, g_p, g_sp, g_dec, g_cum, g_x, g_it, g_m, g_tr, g_zero = tmp
        wgi = at(O_HML, KD, 2, R)
        convw = at(O_CW, CT, TAPS)
        hh = at(O_OH, T, FE)
        sg = at(O_OH + 2 * KIB, T, FE)
        hhT = at(O_OH + 4 * KIB, 2, S)
        wr = at(O_OH + 6 * KIB, KD, E)
        ytmp = xs
        spare_gu = at(O_XT, KD * 512)
        spare_down = at(O_XS, 2 * D)
        ws_down = at(O_NRM, 2, D)
        gate = at(O_QK, T, PASSES * E)
        rk = at(O_QK + 512, T, RKW)
        o_rt = O_QK + 512 + T * RKW
        score = at(o_rt, T, E)
        choice = at(o_rt + 128, E)
        cand = at(o_rt + 192, E)
        top8 = at(o_rt + 256, EG, 8)
        sel = at(o_rt + 320, 4, E)
        zero64 = at(o_rt + 576, E)
        h_part = [nc.alloc_sbuf_tensor_at(f"h_part{i}", [P, T, D], BF16,
                                          offset=arena_at + 4 * (O_XBC + i * T * D // 2)) for i in range(3)]
        h_rest = xs
        onehotb = [nc.alloc_sbuf_tensor_at(f"onehotb{i}", [P, T, 2 * M], BF16,
                                           offset=arena_at + 4 * (O_XBC + 3 * T * D // 2 + i * T * M))
                   for i in range(2)]
        onehot = [at(O_Z + i * 256, T, 2 * M) for i in range(2)]
        onehotT = [rounded(f"onehotT{i}", O_Z + 512 + i * 256, T, P) for i in range(2)]
        psg = at(O_Z + 1024, FE)
        phh = at(O_Z + 1280, FE)
        phhT = at(O_Z + 1536, 2, P)
        iota = at(O_Z + 1792, M)
        gcol = at(O_Z + 1856, 1)
        hc = [at(O_V + i * KD * P, KD, P) for i in range(2)]
        y_hi = rounded("y_hi", O_ST, D)
        y_lo = rounded("y_lo", O_ST + D, D)

        ident = small("ident", [P, P])
        identb = small("identb", [P, P], BF16)
        negm = small("negm", [P, 2, P], BF16)
        zb = small("zb", [P, P], BF16)
        rc = small("rc", [R, RC + FAMS * 4])
        convb = small("convb", [P, CT])
        dsk = small("dsk", [P, SH])
        rbias = small("rbias", [P, E])
        ea = small("ea", [R, 1])
        mcol = small("mcol", [R, 1])
        inic = small("inic", [R, 1])
        g0m = small("g0m", [R, 1])
        em_col = small("em_col", [P, T, 2, H])
        dt_col = small("dt_col", [P, T, 2, SH])
        stat = small("stat", [P, 8, 6])
        mv = small("mv", [P, 8, 2])
        vv = small("vv", [P, 5, 16])
        ssq = small("ssq", [P, T, G])
        dcol = small("dcol", [P, 2])
        gsc = small("gsc", [P, 2, EG])
        gt8 = small("gt8", [P, 8])
        selb = small("selb", [P, T, E], BF16)
        before = small("before", [P, P], BF16)
        onesb = small("onesb", [P, P], BF16)
        rounds_f = small("rounds_f", [P, 2])
        rounds = small("rounds", [1, 1], I32)
        need = small("need", [P, 2])

        s_rc = sem("s_rc")
        s_ident = sem("s_ident")
        s_conv = sem("s_conv")
        s_mask = sem("s_mask")
        s_vec = sem("s_vec")
        oneh_ready = sem("oneh_ready")
        expo_ready = sem("expo_ready")
        s_gatew = [sem(f"s_gatew{i}") for i in range(2)]
        s_late = sem("s_late")
        s_xin = sem("s_xin")
        s_out = sem("s_out")
        s_shared = sem("s_shared")
        s_shdown = sem("s_shdown")
        s_spare_gu = sem("s_spare_gu")
        s_spare_down = sem("s_spare_down")
        slot_gu = [sem(f"slot_gu{i}") for i in range(4)]
        slot_down = [sem(f"slot_down{i}") for i in range(4)]
        unit_full = [sem(f"unit_full{i}") for i in range(RING_U)]
        unit_hi = sem("unit_hi")
        unit_lo = sem("unit_lo")
        x_hi_ready = sem("x_hi_ready")
        x_lo_ready = sem("x_lo_ready")
        mix_used = sem("mix_used")
        s_wr = sem("s_wr")
        pads_ready = sem("pads_ready")
        proj_ready = sem("proj_ready")
        gate_read = sem("gate_read")
        proj_evac = sem("proj_evac")
        gates_z = sem("gates_z")
        gates_u = sem("gates_u")
        em_arg = sem("em_arg")
        em_ready = sem("em_ready")
        misc_ready = sem("misc_ready")
        misc_evac = sem("misc_evac")
        conv_done = sem("conv_done")
        conv_silu = sem("conv_silu")
        decay_ready = sem("decay_ready")
        decay_exp = sem("decay_exp")
        weight_ready = sem("weight_ready")
        ml_ready = sem("ml_ready")
        ml_read = sem("ml_read")
        xdt_ready = sem("xdt_ready")
        ssm_ready = sem("ssm_ready")
        ssm_read = sem("ssm_read")
        y_gated = sem("y_gated")
        o_sig = sem("o_sig")
        sq_done = sem("sq_done")
        var_ready = sem("var_ready")
        sqrt_done = sem("sqrt_done")
        y_ready = sem("y_ready")
        h_ready = sem("h_ready")
        logit_ready = sem("logit_ready")
        score_ready = sem("score_ready")
        gates_done = sem("gates_done")
        h_split = sem("h_split")
        sh_gu = sem("sh_gu")
        sh_silu = sem("sh_silu")
        sh_hh = sem("sh_hh")
        sh_tr = sem("sh_tr")
        sh_hhT = sem("sh_hhT")
        sel_bf = sem("sel_bf")
        rank_ready = sem("rank_ready")
        rounds_ready = sem("rounds_ready")
        iota_ready = sem("iota_ready")
        empty_ready = sem("empty_ready")
        onehot_made = sem("onehot_made")
        onehot_ready = sem("onehot_ready")
        gather_ready = sem("gather_ready")
        gathered = sem("gathered")
        slotT_ready = sem("slotT_ready")
        slotT_read = sem("slotT_read")
        gu_ready = sem("gu_ready")
        silu_done = sem("silu_done")
        hidden_ready = sem("hidden_ready")
        hidT_ready = sem("hidT_ready")
        hidT_read = sem("hidT_read")
        down_ready = sem("down_ready")
        yhi_ready = sem("yhi_ready")
        ylo_ready = sem("ylo_ready")
        moe_ready = sem("moe_ready")
        out_ready = sem("out_ready")
        s_dve = sem("s_dve")

        GU = slice(0, KD * 512)
        DOWN = slice(KD * 512, SLOT)
        SPLIT = ((0, 0), (1, 0), (0, 1))

        CPAIR, VSTEP, ZSTEP, OSTEP = 1, 13, 17, 21
        OROWS = ((OSTEP, OSTEP + 1), (OSTEP + 2,), (OSTEP + 3,), ())
        M_COL, M_ST, M_CB, M_XS, M_Y, M_H = 0, 1, 5, 9, 13, 21
        SRC = {(d, t): [b for b, (bd, _, bt, _) in enumerate(BLOCKS) if (bd, bt) == (d, t)]
               for d in range(2) for t in range(T)}

        block = ctx.enter_context(nc.Block())

        @block.sync
        def _(sp):
            sp.dma_start(rc[:], a["rc"]).then_inc(s_rc, 16)
            for i in range(2):
                k = slice(i * KD // 2, (i + 1) * KD // 2)
                sp.dma_start(wgi[:, k], a["wgi"][:, k]).then_inc(s_gatew[i], 16)
                sp.dma_start(xT[:, k], a["xT"][:, k]).then_inc(s_gatew[i], 16)
            sp.dma_start(ident[:], a["ident"]).then_inc(s_ident, 16)
            for u in range(UNITS):
                if u == RING_U:
                    sp.dma_start(at(O_CW, CT * TAPS), a["convw"]).then_inc(s_conv, 16)
                    sp.dma_start(convb[:], a["convb"]).then_inc(s_conv, 16)
                if u >= RING_U:
                    if u - RING_U < CUNITS + RUNITS:
                        sp.wait_ge(proj_ready, u - RING_U + 2)
                    else:
                        sp.wait_ge(mix_used, u - RING_U - CUNITS - RUNITS + 1)
                if u < CUNITS:
                    src = a["wc"][u]
                elif u < CUNITS + RUNITS:
                    src = a["wn"][u - CUNITS]
                else:
                    c = (u - CUNITS - RUNITS) * UNIT
                    src = a["wo"][:, c:c + UNIT]
                sp.dma_start(unit[u % RING_U], src).then_inc(unit_full[u % RING_U], 16)

            sp.wait_ge(mix_used, OUNITS - 2)
            sp.dma_start(slot[SHARED_SLOT][:, GU], a["ws"][:, GU]).then_inc(s_shared, 16)
            sp.dma_start(at(O_NRM, 2 * D), a["ws"][:, DOWN]).then_inc(s_shdown, 16)

            def load(s, e, part, full):
                src = a["we"][e] if isinstance(e, int) else a["we"][bass.ds(e, 1)].rearrange("o p n -> (o p) n")
                sp.dma_start(slot[s][:, part], src[:, part]).then_inc(full[s], 16)

            sp.wait_ge(mix_used, OUNITS)
            for part, full in ((GU, slot_gu), (DOWN, slot_down)):
                for e in range(2):
                    load(PAIR_SLOTS[0][e], e, part, full)
            for part, full in ((GU, slot_gu), (DOWN, slot_down)):
                load(1, 3, part, full)
            sp.wait_ge(sh_gu, T)
            for part, full in ((GU, slot_gu), (DOWN, slot_down)):
                load(SHARED_SLOT, 2, part, full)
            sp.wait_ge(h_ready, T)
            sp.dma_start(spare_gu, a["we"][SPARE][:, GU]).then_inc(s_spare_gu, 16)
            sp.wait_ge(h_split, 4)
            sp.dma_start(spare_down, a["we"][SPARE][:, DOWN]).then_inc(s_spare_down, 16)

            def load_round(j):
                for v in range(2):
                    experts = [(PAIR_SLOTS[v][e], (j * 4 + (2 * v + e)) % E) for e in range(2)]
                    experts = [(s, e) for s, e in experts if not (isinstance(e, int) and e == SPARE)]
                    sp.wait_ge(gu_ready, j * 2 + (v - 1))
                    for s, e in experts:
                        load(s, e, GU, slot_gu)
                    sp.wait_ge(down_ready, j * 4 + (2 * v - 2))
                    for s, e in experts:
                        load(s, e, DOWN, slot_down)

            load_round(1)
            sp.wait_ge(rounds_ready, 1)
            n_rounds = sp.value_load(rounds[0:1, 0:1], min_val=PAIRS // 2, max_val=PASSES * PAIRS // 2)
            with sp.Fori(2, n_rounds) as j:
                load_round(j)

            for t in range(T):
                sp.wait_ge(out_ready, t + 1)
                sp.dma_start(out[0, t * P:(t + 1) * P, :], ytmp[:, t, :]).then_inc(s_out, 16)
            sp.wait_ge(s_out, 16 * T)

        @block.gpsimd
        def _(pool):
            pool.dma_start(identb[:], a["ident"]).then_inc(s_mask, 16)
            pool.dma_start(negm[:], a["negm"]).then_inc(s_mask, 16)

            def low_part(u):
                pool.wait_ge(unit_hi, u + 1)
                hi, lo = unit_part[u % RING_U]
                nc.gpsimd.tensor_tensor(lo[:], unit[u % RING_U], hi[:].bitcast(F32), ALU.subtract).then_inc(unit_lo, 1)

            nc.gpsimd.memset(vext[:, :, :, DV:DV + 1], 1.0).then_inc(pads_ready, 1)
            nc.gpsimd.memset(xpad[:, :, 0:2], 0.0).then_inc(pads_ready, 1)
            nc.gpsimd.memset(xpad[:, :, S + 2:S + 4], 0.0).then_inc(pads_ready, 1)
            nc.gpsimd.memset(zb[:], 0.0).then_inc(pads_ready, 1)
            nc.gpsimd.memset(onesb[:], 1.0).then_inc(pads_ready, 1)
            pool.wait_ge(unit_lo, 1)
            low_part(1)
            pool.dma_start(dsk[:], a["dsk"].to_broadcast([P, SH])).then_inc(s_vec, 16)
            pool.dma_start(rbias[:], a["rbias"].to_broadcast([P, E])).then_inc(s_vec, 16)
            low_part(2)
            pool.dma_start(at(O_NRM, 2 * D), a["nrm"].to_broadcast([P, 2 * D])).then_inc(s_vec, 16)
            pool.dma_start(before[:], a["before"]).then_inc(s_vec, 16)
            low_part(3)
            for u in range(4, UNITS - 2):
                low_part(u)
            pool.wait_ge(weight_ready, NB)
            pool.dma_start(at(O_ST, T * D), a["x"]).then_inc(s_xin, 16)
            pool.wait_ge(ssm_ready, 2 * G)
            pool.dma_start(at(O_XPAD, 4 * D), a["ln"].to_broadcast([P, 4 * D])).then_inc(s_late, 16)
            for u in range(UNITS - 2, UNITS):
                low_part(u)
            pool.wait_ge(y_gated, T)
            pool.dma_start(wr, a["wr"]).then_inc(s_wr, 16)
            nc.gpsimd.iota(iota, [[1, M]], base=0, channel_multiplier=0,
                           allow_small_or_imprecise_dtypes=True).then_inc(iota_ready, 1)

            def shared_hidden(t):
                pool.wait_ge(sh_silu, t + 1)
                nc.gpsimd.tensor_tensor(hh[:, t, :], sg[:, t, :], hh[:, t, :], ALU.mult).then_inc(sh_hh, 1)

            shared_hidden(0)
            pool.wait_ge(h_split, 1)
            nc.gpsimd.tensor_tensor(h_rest[:], h[:], h_part[0][:], ALU.subtract).then_inc(h_split, 1)
            pool.wait_ge(h_split, 3)
            nc.gpsimd.tensor_tensor(h_part[2][:], h_rest[:], h_part[1][:], ALU.subtract).then_inc(h_split, 1)
            shared_hidden(1)
            pool.wait_ge(s_spare_gu, 16)
            pool.wait_ge(gu_ready, 1)
            nc.gpsimd.tensor_copy(slot[PAIR_SLOTS[0][0]][:, GU], spare_gu).then_inc(slot_gu[PAIR_SLOTS[0][0]], 16)
            pool.wait_ge(s_spare_down, 16)
            pool.wait_ge(down_ready, 2)
            nc.gpsimd.tensor_copy(slot[PAIR_SLOTS[0][0]][:, DOWN], spare_down
                                  ).then_inc(slot_down[PAIR_SLOTS[0][0]], 16)

        @block.tensor
        def _(pe):
            def bank_free(n):
                if n == 2:
                    pe.wait_ge(gate_read, 1)
                elif n > 2:
                    pe.wait_ge(proj_evac, n - 2)

            def misc(m):
                if m >= 2:
                    pe.wait_ge(misc_evac, m - 1)
                return bank[4 + m % 2]

            def project_unit(n, fam=None):
                bank_free(n)
                u = n - 1
                pe.wait_ge(unit_lo, u + 1)
                if fam == 0:
                    pe.wait_ge(oneh_ready, 1)
                    pe.wait_ge(expo_ready, 1)
                    pe.wait_ge(s_mask, 32)
                for j in range(2):
                    for i, (wp, xp) in enumerate(SPLIT):
                        if n == CPAIR and j == 0 and i != 1:
                            pe.wait_ge(x_lo_ready if xp else x_hi_ready, 1)
                        w, x = unit_part[u % RING_U][wp], x_part[xp]
                        for k in range(KD):
                            if u < CUNITS:
                                wk = w[:, (j * KD + k) * P:(j * KD + k + 1) * P]
                                xk = x[:, k, :]
                            else:
                                wk = x[:, k, j * P:(j + 1) * P]
                                xk = w[:, k * S:(k + 1) * S]
                            mm = nc.tensor.matmul(bank[n % 2][:, j * S:(j + 1) * S], wk, xk,
                                                  start=(i == 0 and k == 0), stop=(i == 2 and k == KD - 1))
                        if j == 1 and i == 2:
                            mm.then_inc(proj_ready, 1)
                        if fam is not None:
                            decay_block(fam, 3 * j + i)

            def decay_block(fam, b):
                d, s, t, diag = BLOCKS[b]
                n = fam * NB + b
                r = slice(RD * d, RD * (d + 1))
                ps = bank[2 + n % 2]
                if n >= 2:
                    pe.wait_ge(weight_ready, n - 1)
                for j in range(4):
                    nc.tensor.matmul(ps[:, j * P:(j + 1) * P], oneh[r, 4 * fam + j, :],
                                     expo[r, 2, t * P:(t + 1) * P], start=(j == 0), stop=False,
                                     skip_group_check=True)
                if diag:
                    nc.tensor.matmul(ps[:, :].rearrange("p (j t) -> p j t", j=4), identb[:],
                                     negm[:, d:d + 1, :].to_broadcast([P, 4, P]), start=False, stop=False,
                                     skip_group_check=True)
                mm = nc.tensor.matmul(ps[:, :], expo[r, 0 if diag else 1, s * P:(s + 1) * P],
                                      oneh[r, 4 * fam:4 * fam + 4, :], start=False, stop=True,
                                      skip_group_check=True)
                mm.then_inc(decay_ready, 1)

            for k in range(KD):
                if k % (KD // 2) == 0:
                    pe.wait_ge(s_gatew[k // (KD // 2)], 32)
                for j in range(2):
                    mm = nc.tensor.matmul(bank[6 * j][:, 0:S], wgi[:, k, j, :], xT[:, k, :],
                                          start=(k == 0), stop=(k == KD - 1))
            mm.then_inc(proj_ready, 1)
            for n in range(CPAIR, CPAIR + 4):
                project_unit(n)
            for n in range(CPAIR + 4, CPAIR + 8):
                project_unit(n)
                if n == CPAIR + 4:
                    pe.wait_ge(s_ident, 16)
                    pe.wait_ge(em_ready, 1)
                    ps = misc(M_COL)
                    for i, src in enumerate((g_tr, g_sp)):
                        for t in range(T):
                            mm = nc.tensor.transpose(ps[:, (2 * i + t) * P:(2 * i + t + 1) * P],
                                                     src[:, t * P:(t + 1) * P], ident[:])
                    mm.then_inc(misc_ready, 1)
            pe.wait_ge(proj_evac, 4)
            for hd in range(H):
                ps = misc(M_ST + hd)
                for s in range(T):
                    mm = nc.tensor.matmul(ps[:, s * S:(s + 1) * S], kT[:, hd, s * P:(s + 1) * P], qT[:, hd, :],
                                          start=True, stop=True)
                mm.then_inc(misc_ready, 1)
            for n in range(CPAIR + 8, VSTEP):
                project_unit(n)
            for n in range(VSTEP, ZSTEP):
                project_unit(n)
            pe.wait_ge(conv_silu, 4)
            for g in range(G):
                ps = misc(M_CB + g)
                for s in range(T):
                    mm = nc.tensor.matmul(ps[:, s * S:(s + 1) * S], xbc[:, g, s * P:(s + 1) * P],
                                          xbc[:, G + g, :], start=True, stop=True)
                mm.then_inc(misc_ready, 1)
            pe.wait_ge(conv_silu, 8)
            for m in range(4):
                ps = misc(M_XS + m)
                t, half = m // 2, m % 2
                for j in range(4):
                    mm = nc.tensor.transpose(ps[:, j * P:(j + 1) * P],
                                             xbc[:, 8 + 4 * half + j, t * P:(t + 1) * P], ident[:])
                mm.then_inc(misc_ready, 1)
            n = 0
            for t in range(T):
                for hd in range(H):
                    if hd % 2 == 0:
                        z = 2 * t + hd // 2
                        project_unit(ZSTEP + z, {0: 0, 3: 1}.get(z))
                    if n == 0:
                        pe.wait_ge(pads_ready, 5)
                        pe.wait_ge(proj_evac, ZSTEP - 1)
                        pe.wait_ge(weight_ready, NB)
                    for d in range(2):
                        if n >= 2:
                            pe.wait_ge(ml_read, n - 1)
                        for j, b in enumerate(SRC[d, t]):
                            mm = nc.tensor.matmul(bank[6 + n % 2][:, 0:DV + 1], W[0][b][:, hd, :],
                                                  vext[:, BLOCKS[b][1], hd, :], start=(j == 0),
                                                  stop=(j == len(SRC[d, t]) - 1))
                        mm.then_inc(ml_ready, 1)
                        n += 1
            for g in range(G):
                fam = 1 + g
                for i, n in enumerate(OROWS[g]):
                    project_unit(n, fam + 1 if i == 0 else None)
                pe.wait_ge(weight_ready, (fam + 1) * NB)
                pe.wait_ge(xdt_ready, 4)
                for t in range(T):
                    if g == 0:
                        pe.wait_ge(ml_read, 16)
                    else:
                        pe.wait_ge(ssm_read, 2 * (g - 1) + t + 1)
                    for j in range(4):
                        parts = [(d, b) for d in range(2) for b in SRC[d, t]]
                        for i, (d, b) in enumerate(parts):
                            col = (4 * g + j) * HP
                            mm = nc.tensor.matmul(bank[6 + t][:, j * HP:(j + 1) * HP], W[fam % 2][b][:, j, :],
                                                  xdt[:, d, BLOCKS[b][1], col:col + HP], start=(i == 0),
                                                  stop=(i == len(parts) - 1))
                    mm.then_inc(ssm_ready, 1)
            def y_transpose(m):
                if m % 4 == 0:
                    pe.wait_ge(y_ready, 1 + m // 4)
                ps = misc(M_Y + m)
                for c in range(2):
                    for t in range(T):
                        col = (2 * m + c) % 8 * P
                        mm = nc.tensor.transpose(ps[:, (2 * c + t) * P:(2 * c + t + 1) * P],
                                                 (hml if m < 4 else xs)[:, t, col:col + P], ident[:])
                mm.then_inc(misc_ready, 1)

            def project(k, t):
                if k % 2 == 0 and t == 0:
                    pe.wait_ge(misc_evac, M_Y + k // 2 + 1)
                    pe.wait_ge(unit_lo, CUNITS + RUNITS + k // 2 + 1)
                for i, (wp, yp) in enumerate(SPLIT):
                    w = unit_part[(CUNITS + RUNITS + k // 2) % RING_U][wp]
                    for half in range(2):
                        c = k % 2 * D + half * 512
                        mm = nc.tensor.matmul(bank[2 * t + half][:, :], y_part[yp][:, k, t * P:(t + 1) * P],
                                              w[:, c:c + 512], start=(k == 0 and i == 0),
                                              stop=(k == 2 * KD - 1 and i == 2))
                return mm

            for m in range(4):
                y_transpose(m)
            pe.wait_ge(proj_evac, OSTEP + 3)
            pe.wait_ge(weight_ready, 5 * NB)
            for k in range(12):
                if k == KD:
                    y_transpose(4)
                    y_transpose(5)
                for t in range(T):
                    mm = project(k, t)
                if k % 2 == 1:
                    mm.then_inc(mix_used, 1)
                if k in (KD + 1, KD + 3):
                    y_transpose(k // 2 + 2)
            for t in range(T):
                for k in range(12, 2 * KD):
                    mm = project(k, t)
                mm.then_inc(mix_used, 1)
            wgu = slot[SHARED_SLOT][:, GU].rearrange("p (k c) -> p k c", c=512)
            for t in range(T):
                pe.wait_ge(h_ready, t + 1)
                for half in range(2):
                    ps = misc(M_H + 2 * t + half)
                    for c in range(4):
                        mm = nc.tensor.transpose(ps[:, c * P:(c + 1) * P],
                                                 h[:, t, (4 * half + c) * P:(4 * half + c + 1) * P], ident[:])
                    mm.then_inc(misc_ready, 1)
                pe.wait_ge(misc_evac, M_H + 2 * t + 2)
                if t == 0:
                    pe.wait_ge(s_wr, 16)
                    pe.wait_ge(s_shared, 16)
                else:
                    pe.wait_ge(score_ready, 1)
                for k in range(KD):
                    mm = nc.tensor.matmul(bank[6][:, t * E:(t + 1) * E], hT[:, k, t * P:(t + 1) * P],
                                          wr[:, k, :], start=(k == 0), stop=(k == KD - 1))
                mm.then_inc(logit_ready, 1)
                for k in range(KD):
                    mm = nc.tensor.matmul(bank[t][:, :], hT[:, k, t * P:(t + 1) * P], wgu[:, k, :],
                                          start=(k == 0), stop=(k == KD - 1))
                mm.then_inc(sh_gu, 1)

            pe.wait_ge(s_vec, 64)
            for t in range(T):
                pe.wait_ge(sel_bf, t + 1)
            for t in range(T):
                for i in range(t + 1):
                    nc.tensor.matmul(bank[3][:, 128 + t * E:128 + (t + 1) * E], (before if i == t else onesb)[:],
                                     selb[:, i, :], start=(i == 0), stop=(i == t))
            for i in range(T):
                mm = nc.tensor.matmul(bank[3][:, 256:256 + E], onesb[:], selb[:, i, :],
                                      start=(i == 0), stop=(i == T - 1))
            mm.then_inc(rank_ready, 1)
            pe.wait_ge(score_ready, 2)
            for i in range(4):
                nc.tensor.matmul(bank[4 + i][:, :], zb[:], zb[:, 0:1].to_broadcast([P, 512]),
                                 start=True, stop=False, skip_group_check=True)
            for t in range(T):
                pe.wait_ge(sh_hh, t + 1)
                for f in range(2):
                    mm = nc.tensor.transpose(bank[2][:, (2 * f + t) * P:(2 * f + t + 1) * P],
                                             hh[:, t, f * P:(f + 1) * P], ident[:])
            mm.then_inc(sh_tr, 1)

            def shared_down():
                pe.wait_ge(s_shdown, 16)
                for f in range(2):
                    for t in range(T):
                        for half in range(2):
                            nc.tensor.matmul(bank[4 + 2 * t + half][:, :], hhT[:, f, t * P:(t + 1) * P],
                                             ws_down[:, f, half * 512:(half + 1) * 512],
                                             start=False, stop=False, skip_group_check=True)

            def gather(p1, v, half):
                for k in range(4 * half, 4 * half + 4):
                    for t in range(T):
                        for i in range(3):
                            mm = nc.tensor.matmul(bank[1][:, (k % 4) * P:(k % 4 + 1) * P],
                                                  h_part[i][:, t, k * P:(k + 1) * P], onehotb[v][:, t, :],
                                                  start=(t == 0 and i == 0), stop=(t == T - 1 and i == 2))
                mm.then_inc(gather_ready, 1)

            def scatter(t, last):
                for part in (y_hi, y_lo):
                    for half in range(2):
                        nc.tensor.matmul(bank[4 + 2 * t + half][:, :], onehotT[last][:, t, :],
                                         part[:, half * 512:(half + 1) * 512],
                                         start=False, stop=False, skip_group_check=True)

            pe.wait_ge(h_split, 4)
            pe.wait_ge(onehot_ready, 1)
            gather(0, 0, 0)
            pe.wait_ge(gathered, 1)
            gather(0, 0, 1)
            pe.wait_ge(empty_ready, 1)
            pe.wait_ge(sh_hhT, 1)
            pe.wait_ge(rounds_ready, 1)
            n_rounds = pe.value_load(rounds[0:1, 0:1], min_val=PAIRS // 2, max_val=PASSES * PAIRS // 2)

            def two_pairs(j):
                for v in range(2):
                    p = j * 2 + v
                    pe.wait_ge(onehot_ready, p + 2)
                    pe.wait_ge(gathered, p * 2 + 2)
                    pe.wait_ge(hidT_read, p + 1)
                    gather(p + 1, 1 - v, 0)
                    pe.wait_ge(hidden_ready, p + 1)
                    for e in range(2):
                        s = PAIR_SLOTS[v][e]
                        pe.wait_ge(slot_gu[s], (j + 1) * 16)
                    for k in range(KD):
                        for e in range(2):
                            wk = slot[PAIR_SLOTS[v][e]][:, k * 512:(k + 1) * 512]
                            mm = nc.tensor.matmul(bank[0][e * M:(e + 1) * M, :], hc[v][:, k, e * M:(e + 1) * M], wk,
                                                  start=(k == 0), stop=(k == KD - 1))
                        if k == 2:
                            pe.wait_ge(gathered, p * 2 + 3)
                            gather(p + 1, 1 - v, 1)
                        if k == 5:
                            pe.wait_ge(gathered, p * 2 + 4)
                            for t in range(T):
                                nc.tensor.transpose(bank[1][:, t * P:(t + 1) * P],
                                                    onehot[v][:, t, :], ident[:])
                            for t in range(T):
                                tr = nc.tensor.matmul(bank[1][:, 256:258], onehot[v][:, t, :],
                                                      gate[:, t, bass.ds(p * 2, 2)], start=(t == 0), stop=(t == T - 1))
                            tr.then_inc(slotT_ready, 1)
                    mm.then_inc(gu_ready, 1)
                    pe.wait_ge(ylo_ready, p * 2 + 2)
                    scatter(0, 1 - v)
                    pe.wait_ge(slotT_read, p + 1)
                    pe.wait_ge(hidden_ready, p + 2)
                    for f in range(2):
                        mm = nc.tensor.transpose(bank[1][:, f * P:(f + 1) * P], phh[:, f * P:(f + 1) * P], ident[:])
                    mm.then_inc(hidT_ready, 1)
                    scatter(1, 1 - v)
                    pe.wait_ge(hidT_read, p + 2)
                    for e in range(2):
                        pe.wait_ge(slot_down[PAIR_SLOTS[v][e]], (j + 1) * 16)
                    for half in range(2):
                        for f in range(2):
                            for e in range(2):
                                c = KD * 512 + f * D + half * 512
                                mm = nc.tensor.matmul(bank[2 + half][e * M:(e + 1) * M, :],
                                                      phhT[:, f, e * M:(e + 1) * M],
                                                      slot[PAIR_SLOTS[v][e]][:, c:c + 512],
                                                      start=(f == 0), stop=(f == 1))
                        mm.then_inc(down_ready, 1)

            with pe.Fori(0, FIRST_ROUNDS) as j:
                two_pairs(j)
            shared_down()
            with pe.Fori(FIRST_ROUNDS, n_rounds) as j:
                two_pairs(j)
            pe.wait_ge(ylo_ready, n_rounds * 4 + 2)
            for t in range(T):
                scatter(t, 1)
                for half in range(2):
                    mm = nc.tensor.matmul(bank[4 + 2 * t + half][:, :], zb[:], zb[:, 0:1].to_broadcast([P, 512]),
                                          start=False, stop=True, skip_group_check=True)
                mm.then_inc(moe_ready, 1)

        @block.scalar
        def _(act):
            def high_part(u):
                act.wait_ge(unit_full[u % RING_U], 16 * (u // RING_U + 1))
                nc.scalar.activation(unit_part[u % RING_U][0][:], unit[u % RING_U], ACT.Copy).then_inc(unit_hi, 1)

            for u in range(3):
                high_part(u)
            act.wait_ge(s_rc, 16)
            act.wait_ge(gates_z, 1)
            nc.scalar.activation(g_u, g_nz, ACT.Exp).then_inc(gates_u, 1)
            nc.scalar.activation(ea[:], rc[:, 2:3], ACT.Exp).then_inc(gates_u, 1)

            def evac(n, dst, src, scale=1.0, func=ACT.Copy):
                act.wait_ge(proj_ready, n + 1)
                nc.scalar.activation(dst, src, func, scale=scale).then_inc(proj_evac, 1)
                high_part(n + 2)

            def pair(n):
                return bank[n % 2][:, :].rearrange("p (j t) -> p j t", j=2)

            evac(1, qT[:, 0:2, :], pair(1))
            evac(2, qT[:, 2:4, :], pair(2))
            evac(3, kT[:, 0:2, :], pair(3), scale=DQK ** -0.5)
            evac(4, kT[:, 2:4, :], pair(4), scale=DQK ** -0.5)
            act.wait_ge(em_arg, 1)
            nc.scalar.activation(g_tr, g_m, ACT.Exp).then_inc(em_ready, 1)
            act.wait_ge(pads_ready, 5)
            for n in range(CPAIR + 4, VSTEP):
                c = 2 * (n - CPAIR - 4)
                evac(n, xpad[:, c:c + 2, 2:S + 2], pair(n))

            def conv_act(m):
                act.wait_ge(conv_done, 2 * m + 2)
                nc.scalar.activation(xbc[:, 2 * m:2 * m + 2, :], xbc[:, 2 * m:2 * m + 2, :],
                                     ACT.Silu).then_inc(conv_silu, 1)

            def decay_exps(fam):
                for n in range(fam * NB, (fam + 1) * NB):
                    act.wait_ge(decay_ready, n + 1)
                    ps = bank[2 + n % 2]
                    nc.scalar.activation(ps[:, :], ps[:, :], ACT.Exp).then_inc(decay_exp, 1)

            for m in range(4):
                conv_act(m)
            for n in range(VSTEP, ZSTEP):
                evac(n, vext[:, :, n - VSTEP, 0:DV], pair(n))
                conv_act(4 + n - VSTEP)
            for n in range(ZSTEP, OSTEP):
                if n == ZSTEP:
                    decay_exps(0)
                if n == OSTEP - 1:
                    decay_exps(1)
                evac(n, zs[:, :, (n - ZSTEP) * S:(n - ZSTEP + 1) * S], pair(n), func=ACT.Silu)
            act.wait_ge(ml_ready, 16)
            for g in range(G):
                if g < G - 1:
                    decay_exps(g + 2)
                for n in OROWS[g]:
                    evac(n, osig[:, :, (n - OSTEP) * S:(n - OSTEP + 1) * S], pair(n))
                if g == 0:
                    act.wait_ge(var_ready, 1)
                    nc.scalar.activation(vv[:, 1, 0:8], vv[:, 0, 0:8], ACT.Sqrt).then_inc(sqrt_done, 1)
            act.wait_ge(proj_evac, OSTEP + 3)
            nc.scalar.activation(at(O_V, T * D), at(O_V, T * D), ACT.Sigmoid).then_inc(o_sig, 1)
            high_part(CUNITS + RUNITS + 3)
            for t in range(T):
                act.wait_ge(y_gated, t + 1)
                for g in range(G):
                    sq = nc.scalar.activation(bank[7][:, 0:256], xs[:, t, g * 256:(g + 1) * 256], ACT.Square,
                                              accum_out=ssq[:, t, g:g + 1])
                    sq.then_inc(sq_done, 1)
                    act.wait_ge(sq_done, t * G + g + 1)
            def h_copy(t):
                for half in range(2):
                    m = M_H + 2 * t + half
                    act.wait_ge(misc_ready, m + 1)
                    nc.scalar.activation(hT[:, 4 * half:4 * half + 4, t * P:(t + 1) * P],
                                         bank[4 + m % 2][:, :].rearrange("p (k t) -> p k t", k=4), ACT.Copy
                                         ).then_inc(misc_evac, 1)

            def roots(c, count):
                act.wait_ge(var_ready, count)
                nc.scalar.activation(vv[:, 1, c], vv[:, 0, c], ACT.Sqrt).then_inc(sqrt_done, 1)

            def route_score(t):
                act.wait_ge(logit_ready, t + 1)
                nc.scalar.activation(score[:, t, :], bank[6][:, t * E:(t + 1) * E], ACT.Sigmoid
                                     ).then_inc(score_ready, 1)

            def shared_gate(t):
                act.wait_ge(sh_gu, t + 1)
                nc.scalar.activation(sg[:, t, :], bank[t][:, 0:FE], ACT.Silu)
                nc.scalar.activation(hh[:, t, :], bank[t][:, FE:2 * FE], ACT.Copy).then_inc(sh_silu, 1)

            roots(slice(8, 16), 2)
            for u in range(CUNITS + RUNITS + 4, UNITS):
                high_part(u)
            roots(slice(0, 1), 3)
            h_copy(0)
            roots(slice(1, 2), 4)
            route_score(0)
            shared_gate(0)
            h_copy(1)
            act.wait_ge(h_ready, T)
            nc.scalar.activation(h_part[0][:], h[:], ACT.Copy).then_inc(h_split, 1)
            route_score(1)
            act.wait_ge(h_split, 2)
            nc.scalar.activation(h_part[1][:], h_rest[:], ACT.Copy).then_inc(h_split, 1)
            shared_gate(1)
            act.wait_ge(sh_tr, 1)
            nc.scalar.activation(hhT[:], bank[2][:, :].rearrange("p (f t) -> p f t", f=2), ACT.Copy
                                 ).then_inc(sh_hhT, 1)
            nc.scalar.activation(y_hi[:], zb[:, 0:1].to_broadcast([P, D]), ACT.Copy).then_inc(yhi_ready, 1)

            def gather_copy(n, v, half):
                act.wait_ge(gather_ready, n)
                nc.scalar.activation(hc[v][:, 4 * half:4 * half + 4, :],
                                     bank[1][:, :].rearrange("p (k c) -> p k c", k=4), ACT.Copy).then_inc(gathered, 1)

            gather_copy(1, 0, 0)
            gather_copy(2, 0, 1)
            act.wait_ge(rounds_ready, 1)
            n_rounds = act.value_load(rounds[0:1, 0:1], min_val=PAIRS // 2, max_val=PASSES * PAIRS // 2)
            with act.Fori(0, n_rounds) as j:
                for v in range(2):
                    p = j * 2 + v
                    gather_copy(p * 2 + 3, 1 - v, 0)
                    gather_copy(p * 2 + 4, 1 - v, 1)
                    act.wait_ge(gu_ready, p + 1)
                    act.wait_ge(hidden_ready, p + 1)
                    nc.scalar.activation(psg, bank[0][:, 0:FE], ACT.Silu).then_inc(silu_done, 1)
                    for half in range(2):
                        act.wait_ge(down_ready, p * 2 + (half + 1))
                        nc.scalar.activation(y_hi[:, half * 512:(half + 1) * 512], bank[2 + half][:, :],
                                             ACT.Copy).then_inc(yhi_ready, 1)
            for t in range(T):
                act.wait_ge(var_ready, 5 + t)
                nc.scalar.activation(vv[:, 1, t:t + 1], vv[:, 0, t:t + 1], ACT.Sqrt).then_inc(sqrt_done, 1)

        @block.vector
        def _(dve):
            V = nc.vector
            chain = [0]

            def link(ins):
                ins.then_inc(s_dve, 1)
                chain[0] += 1
                dve.wait_ge(s_dve, chain[0])

            for i in range(2):
                dve.wait_ge(s_gatew[i], 32)
                k = slice(i * KD // 2, (i + 1) * KD // 2)
                ins = V.tensor_copy(x_part[0][:, k, :], xT[:, k, :])
            ins.then_inc(x_hi_ready, 1)
            dve.wait_ge(x_hi_ready, 1)
            dve.wait_ge(unit_hi, 1)
            V.tensor_tensor(unit_part[0][1][:], unit[0], unit_part[0][0][:].bitcast(F32),
                            ALU.subtract).then_inc(unit_lo, 1)
            dve.wait_ge(proj_ready, 1)
            V.tensor_tensor(x_part[1][:], xT, x_part[0][:].bitcast(F32), ALU.subtract).then_inc(x_lo_ready, 1)
            dve.wait_ge(s_rc, 16)
            link(V.tensor_scalar(g_z, bank[0][0:R, 0:S], rc[:, 0:1], rc[:, 1:2], ALU.add, ALU.mult))
            V.tensor_scalar(g_it, bank[6][:, 0:S], rc[:, 7:8], None, ALU.add).then_inc(gate_read, 1)
            V.scalar_tensor_tensor(out=g_nz, in0=g_z, scalar=-1.0, in1=g_z, op0=ALU.mult,
                                   op1=ALU.min).then_inc(gates_z, 1)
            link(V.memset(g_zero, 0.0))
            dve.wait_ge(gates_u, 2)
            link(V.tensor_scalar(g_w, g_u, 2.0, None, ALU.add))
            link(V.reciprocal(g_r, g_w))
            link(V.tensor_tensor(g_s, g_u, g_r, ALU.mult))
            link(V.tensor_tensor(g_s2, g_s, g_s, ALU.mult))
            link(V.tensor_scalar(g_p, g_s2, 1.0 / 17.0, None, ALU.mult))
            for k in range(15, 2, -2):
                link(V.scalar_tensor_tensor(out=g_p, in0=g_p, scalar=1.0 / k, in1=g_s2, op0=ALU.add, op1=ALU.mult))
            link(V.scalar_tensor_tensor(out=g_p, in0=g_p, scalar=1.0, in1=g_s, op0=ALU.add, op1=ALU.mult))
            link(V.tensor_scalar(g_w, g_z, 0.0, None, ALU.max))
            link(V.scalar_tensor_tensor(out=g_sp, in0=g_p, scalar=2.0, in1=g_w, op0=ALU.mult, op1=ALU.add))
            link(V.tensor_scalar(mcol[:], ea[:], -1.0, None, ALU.mult))
            link(V.tensor_scalar(g_dec, g_sp, mcol[:], None, ALU.mult))
            link(V.tensor_tensor_scan(g_cum[:, 0:P], g_dec[:, 0:P], g_zero[:, 0:P], 0.0, ALU.add, ALU.add))
            link(V.tensor_tensor(inic[:], g_cum[:, P - 1:P], rc[:, 5:6], ALU.mult))
            link(V.tensor_tensor_scan(g_cum[:, P:S], g_dec[:, P:S], g_zero[:, P:S], inic[:], ALU.add, ALU.add))
            link(V.tensor_scalar(g_x, g_cum, rc[:, 3:4], None, ALU.mult))
            link(V.scalar_tensor_tensor(out=g_x, in0=g_dec, scalar=rc[:, 4:5], in1=g_x, op0=ALU.mult, op1=ALU.add))
            link(V.tensor_tensor(g0m[:], g_cum[:, P - 1:P], rc[:, 6:7], ALU.mult))
            link(V.tensor_tensor(col_d, g_it, g_x, ALU.subtract))
            link(V.tensor_scalar(col_o, col_d, g0m[:], None, ALU.add))
            link(V.tensor_tensor_scan(g_m[0:RD, :], col_d[0:RD, :], col_d[0:RD, :], NEG, ALU.max, ALU.max))
            link(V.tensor_tensor_scan(g_m[RD:R, ::-1], col_d[RD:R, ::-1], col_d[RD:R, ::-1], NEG, ALU.max,
                                      ALU.max))
            link(V.tensor_scalar(g_w, g_m, rc[:, 5:6], -1.0, ALU.mult, ALU.mult))
            link(V.scalar_tensor_tensor(out=row_t, in0=g_x, scalar=rc[:, 6:7], in1=g_w, op0=ALU.mult, op1=ALU.add))
            V.tensor_tensor(g_m, row_t, g_x, ALU.subtract).then_inc(em_arg, 1)
            dve.wait_ge(em_arg, 1)
            for i in range(2):
                link(V.tensor_copy(expo[:], exact))
                link(V.scalar_tensor_tensor(out=exact, in0=expo[:], scalar=rc[:, 8 + i:9 + i], in1=exact,
                                            op0=ALU.mult, op1=ALU.add))
            V.tensor_copy(expo[:], exact).then_inc(expo_ready, 1)
            V.tensor_copy(oneh[:], rc[:, RC:].unsqueeze(2).to_broadcast([P, FAMS * 4, P])).then_inc(oneh_ready, 1)

            def misc_copy(m, dst, src):
                dve.wait_ge(misc_ready, m + 1)
                V.tensor_copy(dst, src).then_inc(misc_evac, 1)

            def mbank(m, n):
                return bank[4 + m % 2][:, :].rearrange("p (j t) -> p j t", j=n)

            def y_split(m):
                hi, lo = (part[:, 2 * m:2 * m + 2, :] for part in y_part)
                dve.wait_ge(misc_ready, M_Y + m + 1)
                link(V.tensor_copy(hi, mbank(M_Y + m, 2)))
                V.tensor_tensor(lo, mbank(M_Y + m, 2), hi.bitcast(F32), ALU.subtract).then_inc(misc_evac, 1)

            def conv(c):
                link(V.tensor_scalar(xbc[:, c, :], xpad[:, c, 0:S], convw[:, c, 0:1], convb[:, c:c + 1],
                                     ALU.mult, ALU.add))
                for k in range(1, TAPS):
                    ins = V.scalar_tensor_tensor(out=xbc[:, c, :], in0=xpad[:, c, k:k + S],
                                                 scalar=convw[:, c, k:k + 1], in1=xbc[:, c, :],
                                                 op0=ALU.mult, op1=ALU.add)
                    if k < TAPS - 1:
                        link(ins)
                ins.then_inc(conv_done, 1)

            def weights(fam):
                if fam == 2:
                    dve.wait_ge(ml_ready, 16)
                elif fam > 2:
                    dve.wait_ge(ssm_ready, 2 * (fam - 2))
                for b, (d, s, t, _) in enumerate(BLOCKS):
                    n = fam * NB + b
                    dve.wait_ge(decay_exp, n + 1)
                    e = bank[2 + n % 2][:, :].rearrange("p (j t) -> p j t", j=4)
                    if fam == 0:
                        sc = st[:, :, s, t * P:(t + 1) * P]
                    else:
                        sc = cb[:, fam - 1, s:s + 1, t * P:(t + 1) * P].to_broadcast([P, 4, P])
                    V.tensor_tensor(W[fam % 2][b], e, sc, ALU.mult).then_inc(weight_ready, 1)

            dve.wait_ge(misc_ready, M_COL + 1)
            cols = bank[4][:, :].rearrange("p (i t d r) -> p i t d r", i=2, t=T, d=2)
            V.tensor_copy(em_col[:], cols[:, 0, :, :, ML0:ML0 + H])
            V.tensor_copy(dt_col[:], cols[:, 1, :, :, 0:SH]).then_inc(misc_evac, 1)
            dve.wait_ge(s_conv, 32)
            for hd in range(H):
                misc_copy(M_ST + hd, st[:, hd, :, :], mbank(M_ST + hd, 2))
            for c in range(CT):
                dve.wait_ge(proj_evac, CPAIR + 4 + c // 2)
                conv(c)
            for g in range(G):
                misc_copy(M_CB + g, cb[:, g, :, :], mbank(M_CB + g, 2))
            for m in range(4):
                misc_copy(M_XS + m, xs[:, m // 2, (m % 2) * 512:(m % 2 + 1) * 512], bank[4 + (M_XS + m) % 2][:, :])
            dve.wait_ge(misc_evac, M_XS + 4)
            dve.wait_ge(s_vec, 64)

            def dt_x(d, t):
                v = xs[:, t, :].rearrange("p (h c) -> p h c", h=SH)
                V.tensor_tensor(xdt[:, d, t, :].rearrange("p (h c) -> p h c", h=SH), v,
                                dt_col[:, t, d, :].unsqueeze(2).to_broadcast([P, SH, HP]),
                                ALU.mult).then_inc(xdt_ready, 1)
            weights(0)
            n = 0
            for t in range(T):
                for hd in range(H):
                    for d in range(2):
                        ps = bank[6 + n % 2]
                        dst = hml[:, t, hd * DV:(hd + 1) * DV]
                        dve.wait_ge(ml_ready, n + 1)
                        link(V.tensor_scalar(dcol[:, 0:1], ps[:, DV:DV + 1], em_col[:, t, d, hd:hd + 1], None, ALU.max))
                        link(V.scalar_tensor_tensor(out=dcol[:, 0:1], in0=ps[:, DV:DV + 1], scalar=-1.0,
                                                    in1=dcol[:, 0:1], op0=ALU.mult, op1=ALU.max))
                        link(V.reciprocal(dcol[:, 1:2], dcol[:, 0:1]))
                        if d == 0:
                            ins = V.tensor_scalar(dst, ps[:, 0:DV], dcol[:, 1:2], None, ALU.mult)
                        else:
                            ins = V.scalar_tensor_tensor(out=dst, in0=ps[:, 0:DV], scalar=dcol[:, 1:2], in1=dst,
                                                         op0=ALU.mult, op1=ALU.add)
                        ins.then_inc(ml_read, 1)
                        n += 1
                        dve.wait_ge(ml_read, n)
                        if n % 4 == 0:
                            dt_x((n // 4 - 1) % 2, (n // 4 - 1) // 2)
                        if n == 12:
                            weights(1)
            def rsqrt(c, count):
                dve.wait_ge(sqrt_done, count)
                link(V.reciprocal(vv[:, 3, c], vv[:, 1, c]))
                link(V.tensor_tensor(vv[:, 4, c], vv[:, 3, c], vv[:, 3, c], ALU.mult))
                link(V.tensor_tensor(vv[:, 4, c], vv[:, 4, c], vv[:, 0, c], ALU.mult))
                link(V.tensor_scalar(vv[:, 4, c], vv[:, 4, c], -0.5, 1.5, ALU.mult, ALU.add))
                link(V.tensor_tensor(vv[:, 3, c], vv[:, 3, c], vv[:, 4, c], ALU.mult))

            for g in range(G):
                if g < G - 1:
                    weights(g + 2)
                    if g == 0:
                        for i in range(8):
                            ins = V.bn_stats(stat[:, i, :], hml[:, i // H, (i % H) * DV:(i % H + 1) * DV])
                        link(ins)
                        for i in range(8):
                            ins = V.bn_aggr(mv[:, i, :], stat[:, i, :])
                        link(ins)
                        V.tensor_scalar(vv[:, 0, 0:8], mv[:, :, 1], EPS, None, ALU.add).then_inc(var_ready, 1)
                        dve.wait_ge(xdt_ready, 4)
                        for t in range(T):
                            v = xs[:, t, :].rearrange("p (h c) -> p h c", h=SH)
                            link(V.tensor_tensor(v, v, dsk[:].unsqueeze(2).to_broadcast([P, SH, HP]), ALU.mult))
                    if g == 1:
                        rsqrt(slice(0, 8), 1)
                        for i in range(8):
                            v = hml[:, i // H, (i % H) * DV:(i % H + 1) * DV]
                            ins = V.tensor_scalar(v, v, mv[:, i, 0:1], vv[:, 3, i:i + 1], ALU.subtract, ALU.mult)
                        link(ins)
                        for t in range(T):
                            link(V.tensor_tensor(hml[:, t, :], hml[:, t, :], nrm[:, 0, :], ALU.mult))
                else:
                    dve.wait_ge(o_sig, 1)
                    for t in range(T):
                        ins = V.tensor_tensor(hml[:, t, :], hml[:, t, :], osig[:, t, :], ALU.mult)
                    ins.then_inc(y_ready, 1)
                    for m in range(4):
                        y_split(m)
                for t in range(T):
                    dve.wait_ge(ssm_ready, 2 * g + t + 1)
                    v = xs[:, t, g * 256:(g + 1) * 256]
                    V.tensor_tensor(v, bank[6 + t][:, 0:256], v, ALU.add).then_inc(ssm_read, 1)
            dve.wait_ge(ssm_read, 2 * G)
            dve.wait_ge(proj_evac, OSTEP - 1)
            for t in range(T):
                V.tensor_tensor(xs[:, t, :], xs[:, t, :], zs[:, t, :], ALU.mult).then_inc(y_gated, 1)

            dve.wait_ge(sq_done, T * G)
            V.tensor_scalar(vv[:, 0, 8:16], ssq[:].rearrange("p t g -> p (t g)"), 1.0 / 256, EPS, ALU.mult,
                            ALU.add).then_inc(var_ready, 1)
            dve.wait_ge(var_ready, 2)
            rsqrt(slice(8, 16), 2)
            for i in range(8):
                v = xs[:, i // G, (i % G) * 256:(i % G + 1) * 256]
                n = nrm[:, 1, (i % G) * 256:(i % G + 1) * 256]
                ins = V.scalar_tensor_tensor(out=v, in0=v, scalar=vv[:, 3, 8 + i:9 + i], in1=n,
                                             op0=ALU.mult, op1=ALU.mult)
            ins.then_inc(y_ready, 1)
            for m in range(4, 8):
                y_split(m)

            def layer_norm(src, dst, which, count, signal, first_bank, summed, used):
                for t in range(T):
                    dve.wait_ge(summed, used[t])
                    for half in range(2):
                        c = slice(half * 512, (half + 1) * 512)
                        link(V.scalar_tensor_tensor(out=dst[:, t, c], in0=src[:, t, c], scalar=ALPHA,
                                                    in1=bank[first_bank + 2 * t + half][:, :],
                                                    op0=ALU.mult, op1=ALU.add))
                        link(V.bn_stats(stat[:, 2 * t + half, :], dst[:, t, c]))
                    link(V.bn_aggr(mv[:, t, :], stat[:, 2 * t:2 * t + 2, :].rearrange("p a b -> p (a b)")))
                    V.tensor_scalar(vv[:, 0, t:t + 1], mv[:, t, 1:2], EPS, None, ALU.add).then_inc(var_ready, 1)
                    dve.wait_ge(var_ready, count + t)
                    v = dst[:, t, :]
                    link(V.scalar_tensor_tensor(out=v, in0=v, scalar=mv[:, t, 0:1], in1=ln[:, 2 * which, :],
                                                op0=ALU.subtract, op1=ALU.mult))
                    rsqrt(slice(t, t + 1), count + t)
                    V.scalar_tensor_tensor(out=v, in0=v, scalar=vv[:, 3, t:t + 1], in1=ln[:, 2 * which + 1, :],
                                           op0=ALU.mult, op1=ALU.add).then_inc(signal, 1)
                dve.wait_ge(signal, T)

            dve.wait_ge(s_xin, 16)
            dve.wait_ge(s_late, 16)
            layer_norm(xin, h, 0, 3, h_ready, 0, mix_used, (OUNITS - 1, OUNITS))
            def top_k(dst, vals, thr, k, w):
                link(V.tensor_scalar(sel[:, 0, 0:w], vals, thr, None, ALU.is_gt, ALU.add, accum_out=need[:, 0:1]))
                link(V.tensor_scalar(need[:, 1:2], need[:, 0:1], -1.0, float(k), ALU.mult, ALU.add))
                link(V.tensor_scalar(sel[:, 1, 0:w], vals, thr, None, ALU.is_equal))
                link(V.tensor_tensor_scan(sel[:, 2, 0:w], sel[:, 1, 0:w], zero64[:, 0:w], 0.0, ALU.add, ALU.add))
                link(V.scalar_tensor_tensor(out=sel[:, 1, 0:w], in0=sel[:, 2, 0:w], scalar=need[:, 1:2],
                                            in1=sel[:, 1, 0:w], op0=ALU.is_le, op1=ALU.mult))
                link(V.tensor_tensor(dst, sel[:, 0, 0:w], sel[:, 1, 0:w], ALU.add))

            dve.wait_ge(s_vec, 64)
            link(V.memset(zero64, 0.0))
            for t in range(T):
                dve.wait_ge(score_ready, t + 1)
                link(V.tensor_tensor(choice, score[:, t, :], rbias[:], ALU.add))
                for g in range(EG):
                    ins = V.max(top8[:, g, :], choice[:, g * 8:(g + 1) * 8])
                link(ins)
                link(V.tensor_tensor(gsc[:, 0, :], top8[:, :, 0], top8[:, :, 1], ALU.add))
                link(V.max(gt8[:], gsc[:, 0, :]))
                top_k(gsc[:, 1, :], gsc[:, 0, :], gt8[:, TOPG - 1:TOPG], TOPG, EG)
                gm = gsc[:, 1, :].unsqueeze(2).to_broadcast([P, EG, 8])
                c3 = cand.rearrange("p (g e) -> p g e", g=EG)
                link(V.tensor_tensor(c3, choice.rearrange("p (g e) -> p g e", g=EG), gm, ALU.mult))
                link(V.tensor_scalar(gsc[:, 0, :], gsc[:, 1, :], BIG, -BIG, ALU.mult, ALU.add))
                link(V.tensor_tensor(c3, c3, gsc[:, 0, :].unsqueeze(2).to_broadcast([P, EG, 8]), ALU.add))
                link(V.max(gt8[:], cand))
                top_k(sel[:, 3, :], cand, gt8[:, TOPK - 1:TOPK], TOPK, E)
                V.tensor_copy(selb[:, t, :], sel[:, 3, :]).then_inc(sel_bf, 1)
                link(V.tensor_tensor(cand, sel[:, 3, :], score[:, t, :], ALU.mult))
                link(V.tensor_reduce(need[:, 0:1], cand, AX_X, ALU.add))
                link(V.reciprocal(need[:, 1:2], need[:, 0:1]))
                for b in range(PASSES):
                    ins = V.tensor_scalar(gate[:, t, b * E:(b + 1) * E], cand, need[:, 1:2], ROUTED_SCALE, ALU.mult,
                                          ALU.mult)
                link(ins)
            dve.wait_ge(rank_ready, 1)
            for t in range(T):
                link(V.tensor_scalar(rk[:, t, 0:E], bank[3][:, 128 + t * E:128 + (t + 1) * E], 1.0, None, ALU.add))
                link(V.tensor_tensor(rk[:, t, 0:E], rk[:, t, 0:E], selb[:, t, :], ALU.mult))
                link(V.tensor_scalar(rk[:, t, 0:E], rk[:, t, 0:E], -1.0, None, ALU.add))

            def one_hot(p, v):
                dst = onehot[v][:, :, :].rearrange("p t (e m) -> p t e m", e=2)
                num = rk[:, :, 2 * p:2 * p + 2] if isinstance(p, int) else rk[:, :, bass.ds(p * 2, 2)]
                V.tensor_tensor(dst, iota.unsqueeze(1).unsqueeze(1).to_broadcast([P, T, 2, M]),
                                num.unsqueeze(3).to_broadcast([P, T, 2, M]), ALU.is_equal).then_inc(onehot_made, 1)
                dve.wait_ge(onehot_made, p + 1)
                V.tensor_copy(onehotb[v][:], onehot[v]).then_inc(onehot_ready, 1)

            dve.wait_ge(iota_ready, 1)
            one_hot(0, 0)
            one_hot(1, 1)
            link(V.tensor_reduce(rounds_f[:, 0:1], bank[3][:, 256:256 + E], AX_X, ALU.max))
            link(V.memset(rounds_f[:, 1:2], PAIRS / 2))
            for b in range(1, PASSES):
                link(V.tensor_scalar(need[:, 0:1], rounds_f[:, 0:1], float(b * M), PAIRS / 2, ALU.is_gt, ALU.mult))
                link(V.tensor_tensor(rounds_f[:, 1:2], rounds_f[:, 1:2], need[:, 0:1], ALU.add))
            V.tensor_copy(rounds[:], rounds_f[0:1, 1:2]).then_inc(rounds_ready, 1)
            for t in range(T):
                for b in range(1, PASSES):
                    V.tensor_scalar(rk[:, t, b * E:(b + 1) * E], rk[:, t, 0:E], -float(b * M), None, ALU.add)
            link(V.memset(rk[:, :, PASSES * E:], -1.0))
            dve.wait_ge(yhi_ready, 1)
            V.memset(onehotT[1][:].bitcast(F32), 0.0).then_inc(empty_ready, 1)
            V.tensor_copy(y_lo[:], y_hi[:].bitcast(F32)).then_inc(ylo_ready, 2)
            V.memset(rounds_f[:, 0:1], 0.0).then_inc(hidT_read, 1)
            V.memset(rounds_f[:, 1:2], 0.0).then_inc(hidden_ready, 1)
            dve.wait_ge(rounds_ready, 1)
            n_rounds = dve.value_load(rounds[0:1, 0:1], min_val=PAIRS // 2, max_val=PASSES * PAIRS // 2)
            with dve.Fori(0, n_rounds) as j:
                for v in range(2):
                    p = j * 2 + v
                    dve.wait_ge(slotT_ready, p + 1)
                    V.tensor_copy(gcol[0:M, :], bank[1][0:M, 256:257])
                    V.tensor_copy(gcol[M:P, :], bank[1][M:P, 257:258])
                    V.tensor_copy(onehotT[v][:], bank[1][:, 0:S].rearrange("p (t s) -> p t s", t=T)
                                  ).then_inc(slotT_read, 1)
                    one_hot(p + 2, v)
                    dve.wait_ge(silu_done, p + 1)
                    dve.wait_ge(slotT_read, p + 1)
                    V.scalar_tensor_tensor(out=phh, in0=psg, scalar=gcol, in1=bank[0][:, FE:2 * FE],
                                           op0=ALU.mult, op1=ALU.mult).then_inc(hidden_ready, 1)
                    dve.wait_ge(hidT_ready, p + 1)
                    V.tensor_copy(phhT, bank[1][:, 0:2 * P].rearrange("p (f s) -> p f s", f=2)).then_inc(hidT_read, 1)
                    for half in range(2):
                        dve.wait_ge(yhi_ready, p * 2 + (half + 2))
                        c = slice(half * 512, (half + 1) * 512)
                        V.tensor_tensor(y_lo[:, c], bank[2 + half][:, :], y_hi[:, c].bitcast(F32),
                                        ALU.subtract).then_inc(ylo_ready, 1)
            layer_norm(h, ytmp, 1, 5, out_ready, 4, moe_ready, (1, 2))


NAMES = ["wgi", "xT", "wc", "wn", "wo", "ws", "we", "before", "rc", "ident", "negm", "convw", "convb", "dsk", "rbias",
         "nrm", "ln", "x", "wr"]


def layout(**v):
    import numpy as np

    f = np.float32
    v = {k: np.asarray(x) for k, x in v.items()}
    x = v["x"][0]
    w = v["w_in"][0]
    q0, k0, v0, o0, i0, f0, z0, c0, d0 = 0, 512, 1024, 2048, 3072, 3080, 3088, 4112, 6160
    rows = lambda m: m.reshape(-1, P, m.shape[1]).transpose(1, 0, 2)
    out = {}
    out["x"] = rows(x).reshape(P, T * D)
    out["xT"] = rows(x.T)
    wgi = np.zeros((D, 2, R), f)
    rc = np.zeros((R, RC + FAMS * 4), f)
    rc[:, 2] = NEG
    for d in range(2):
        for part in range(PARTS):
            m = slice(RD * d + ML0 + H * part, RD * d + ML0 + H * (part + 1))
            s = slice(RD * d + SH * part, RD * d + SH * (part + 1))
            wgi[:, 0, m] = w[:, f0 + d * H:f0 + (d + 1) * H]
            wgi[:, 1, m] = w[:, i0 + d * H:i0 + (d + 1) * H]
            wgi[:, 0, s] = w[:, d0 + d * SH:d0 + (d + 1) * SH]
            rc[m, 0] = v["ml_f_bias"][0, d * H:(d + 1) * H]
            rc[s, 0] = v["dt_bias"][0, d * SH:(d + 1) * SH]
            rc[m, 1], rc[s, 1] = -1, 1
            rc[m, 2] = 0
            rc[s, 2] = v["a_log"][0, d * SH:(d + 1) * SH]
            rc[m, 5] = rc[s, 6] = 1
            rc[m, 7] = v["ml_i_bias"][0, d * H:(d + 1) * H]
            for q in (m, s):
                rc[q, 3] = 1 - 2 * d
                rc[q, 4] = d
                rc[q, 8] = -1 if part >= 1 else 0
                rc[q, 9] = -1 if part == 2 else 0
            for i in range(H):
                rc[m.start + i, RC + i] = 1
            for i in range(SH):
                rc[s.start + i, RC + H + i] = 1
    out["wgi"] = wgi.reshape(KD, P, 2, R).transpose(1, 0, 2, 3)
    out["rc"] = rc
    xbc_order = np.concatenate([np.arange(D, CH), np.arange(D)])
    chans = np.concatenate([np.arange(q0, v0), c0 + xbc_order])
    wc = w[:, chans].reshape(KD, P, CUNITS, 2, P)
    out["wc"] = wc.transpose(2, 1, 3, 0, 4).reshape(CUNITS, P, UNIT)
    wn = np.concatenate([w[:, v0:o0], w[:, z0:c0], w[:, o0:i0]], 1).reshape(KD, P, RUNITS, S)
    out["wn"] = wn.transpose(2, 1, 0, 3).reshape(RUNITS, P, UNIT)
    out["wo"] = rows(v["w_out"][0]).reshape(P, 2 * KD * D)

    def expert(gate, up, down):
        n = gate.shape[0]
        gu = np.concatenate([gate.reshape(n, KD, P, 1, FE), up.reshape(n, KD, P, 1, FE)], 3)
        dn = down.reshape(n, 2, P, D).transpose(0, 2, 1, 3)
        return np.concatenate([gu.transpose(0, 2, 1, 3, 4).reshape(n, P, KD * 512), dn.reshape(n, P, 2 * D)], 2)

    out["ws"] = expert(v["w_sh_gate"], v["w_sh_up"], v["w_sh_down"])[0]
    out["we"] = expert(v["w_exp_gate"][0], v["w_exp_up"][0], v["w_exp_down"][0])
    out["ident"] = np.eye(P, dtype=f)
    s, t = np.arange(P)[:, None], np.arange(P)[None, :]
    out["negm"] = np.stack([np.where(s <= t, 0, NEG), np.where(s >= t, 0, NEG)], 1).astype(f)
    out["before"] = (s < t).astype(f)
    out["convw"] = v["conv_w"][0][:, xbc_order].reshape(TAPS, CT, P).transpose(2, 1, 0).reshape(P, CT * TAPS)
    out["convb"] = v["conv_b"][0][xbc_order].reshape(CT, P).T
    out["dsk"] = v["d_skip"]
    out["rbias"] = v["router_bias"]
    out["nrm"] = np.concatenate([v["ml_norm_w"], v["ssm_norm_w"]], 1)
    out["ln"] = np.concatenate([v["ln1_g"], v["ln1_b"], v["ln2_g"], v["ln2_b"]], 1)
    out["wr"] = rows(v["w_router"][0])
    return {n: np.ascontiguousarray(out[n]) for n in NAMES}


def kernel(**inputs):
    import concourse.bacc as _bacc
    from concourse import mybir as _mybir
    from concourse.bass_utils import run_bass_kernel_spmd as _run

    nc = _bacc.Bacc("TRN2", target_bir_lowering=False, num_devices=1)
    arrays, args = {}, {}
    for name, arr in layout(**inputs).items():
        arrays[f"in_{name}_dram"] = arr
        args[name] = nc.dram_tensor(f"in_{name}_dram", arr.shape, _mybir.dt.from_np(arr.dtype),
                                    kind="ExternalInput").ap()
    out = nc.dram_tensor("out_0_dram", (1, S, D), _mybir.dt.float32, kind="ExternalOutput").ap()
    build(nc, args, out)
    r = _run(nc, [arrays], core_ids=[0])
    return r.results[0]["out_0_dram"]
```
